# Optimizing a Trainium2 kernel written in Bass

```python
import math
import jax, jax.numpy as jnp
from jax import lax
import numpy as np

D_MODEL = 1024
BATCH = 1
SEQ = 256
DEPTH = 2

N_MIXERS = 2
N_RWKV_LAYERS = (DEPTH + 1) // 2
N_ATTN_LAYERS = DEPTH // 2
RMS_EPS = 1e-6
N_MOD = 6

RWKV_HEAD = 64
RWKV_HEADS = D_MODEL // RWKV_HEAD
D_DECAY_LORA = 64
D_AAA_LORA = 64
D_GATE_LORA = 128
RWKV_GN_EPS = 64e-5
N_DIRS = 2
N_SHIFT_MIX = 6

ATTN_GROUPS = ((128, 1), (512, 4), (2048, 16))
N_GROUPS = len(ATTN_GROUPS)
ATTN_HEADS = 8
ATTN_HEAD_DIM = D_MODEL // ATTN_HEADS
QKV_WIDTH = N_GROUPS * 3 * ATTN_HEADS * ATTN_HEAD_DIM
Q_BLOCK = 64
NEG_INF = -1e30

N_EXPERT_GROUPS = 4
EXPERTS_PER_GROUP = 8
TOP_K_INNER = 2
D_EXPERT = D_MODEL // 4


def rms_norm(x, g):
    x32 = x.astype(jnp.float32)
    y = x32 * lax.rsqrt(jnp.mean(x32 * x32, axis=-1, keepdims=True) + RMS_EPS)
    return (y * g.astype(jnp.float32)).astype(x.dtype)

def modulate(h, shift, scale):
    return h * (1.0 + scale[:, None, :]) + shift[:, None, :]

def _wkv7_scan(r, w, k, v, a, b, reverse):
    bsz, _, h, n = r.shape

    def step(state, inp):
        r_t, w_t, k_t, v_t, a_t, b_t = inp
        sa = jnp.einsum('bhvk,bhk->bhv', state, a_t)
        state = (state * w_t[:, :, None, :]
                 + sa[:, :, :, None] * b_t[:, :, None, :]
                 + v_t[:, :, :, None] * k_t[:, :, None, :])
        y_t = jnp.einsum('bhvk,bhk->bhv', state, r_t)
        return state, y_t

    s0 = jnp.zeros((bsz, h, n, n), jnp.float32)
    xs = tuple(jnp.moveaxis(t, 1, 0) for t in (r, w, k, v, a, b))
    _, ys = lax.scan(step, s0, xs, reverse=reverse)
    return jnp.moveaxis(ys, 0, 1)

def rwkv7_mix(h, mu, w_rkv, w0, w1, w2, a0, a1, a2, g1, g2, k_k, k_a, r_k, ln_w, ln_b, w_o):
    bsz, s, d = h.shape
    f32 = jnp.float32
    x_prev = jnp.pad(h, ((0, 0), (1, 0), (0, 0)))[:, :-1]
    x_next = jnp.pad(h, ((0, 0), (0, 1), (0, 0)))[:, 1:]
    xx = 0.5 * (x_prev + x_next) - h
    xs = h[:, :, None, :] + xx[:, :, None, :] * mu
    rkv = jnp.einsum('bsjd,jde->bsje', xs[:, :, :3], w_rkv)
    r, k, v = rkv[:, :, 0], rkv[:, :, 1], rkv[:, :, 2]
    xw, xa, xg = xs[:, :, 3], xs[:, :, 4], xs[:, :, 5]

    def lora(xin, A, Bm, act):
        return jnp.einsum('zbsr,zre->zbse', act(jnp.einsum('bsd,zdr->zbsr', xin, A)), Bm)

    w_log = -jax.nn.softplus(-(w0[:, None, None, :] + lora(xw, w1, w2, jnp.tanh)).astype(f32)) - 0.5
    decay = jnp.exp(-jnp.exp(w_log))
    a = jax.nn.sigmoid((a0[:, None, None, :] + lora(xa, a1, a2, lambda t: t)).astype(f32))
    g = lora(xg, g1, g2, jax.nn.sigmoid).astype(f32)

    def heads(t):
        return t.reshape(t.shape[:-1] + (RWKV_HEADS, RWKV_HEAD))

    r32, k32, v32 = (heads(t.astype(f32)) for t in (r, k, v))
    kk = k32 * heads(k_k.astype(f32))
    kk = kk / jnp.maximum(jnp.sqrt(jnp.sum(kk * kk, axis=-1, keepdims=True)), 1e-12)
    a_h, decay_h = heads(a), heads(decay)
    k_dir = k32[None] * (1.0 + (a_h - 1.0) * heads(k_a.astype(f32)))
    b_dir = kk[None] * a_h
    y_f = _wkv7_scan(r32, decay_h[0], k_dir[0], v32, -kk, b_dir[0], reverse=False)
    y_b = _wkv7_scan(r32, decay_h[1], k_dir[1], v32, -kk, b_dir[1], reverse=True)
    y = jnp.stack([y_f, y_b])
    mean = jnp.mean(y, axis=-1, keepdims=True)
    var = jnp.mean(jnp.square(y - mean), axis=-1, keepdims=True)
    y = (y - mean) * lax.rsqrt(var + RWKV_GN_EPS) * heads(ln_w.astype(f32)) + heads(ln_b.astype(f32))
    bonus = jnp.sum(r32[None] * k_dir * r_k.astype(f32), axis=-1, keepdims=True) * v32[None]
    o = jnp.sum(heads(g) * (y + bonus), axis=0).reshape(bsz, s, d)
    return jnp.einsum('bsd,de->bse', o.astype(h.dtype), w_o)

def alibi_slopes(n):
    return 2.0 ** (-8.0 * jnp.arange(1, n + 1, dtype=jnp.float32) / n)

def _dilated_group(q, k, v, slopes, window, dilation):
    bsz, s, h, dh = q.shape
    half = window // (2 * dilation)
    L = s // dilation
    nb = -(-L // Q_BLOCK)
    lp = nb * Q_BLOCK
    kb_len = Q_BLOCK + 2 * half

    def strided(t):
        return t.reshape(bsz, L, dilation, h, dh).transpose(0, 2, 3, 1, 4)

    qd = jnp.pad(strided(q), ((0, 0), (0, 0), (0, 0), (0, lp - L), (0, 0)))
    qd = qd.reshape(bsz, dilation, h, nb, Q_BLOCK, dh)
    pad_kv = ((0, 0), (0, 0), (0, 0), (half, lp - L + half), (0, 0))
    kd = jnp.pad(strided(k), pad_kv)
    vd = jnp.pad(strided(v), pad_kv)
    key_idx = jnp.arange(nb)[:, None] * Q_BLOCK + jnp.arange(kb_len)[None, :]
    kblk = kd[:, :, :, key_idx]
    vblk = vd[:, :, :, key_idx]
    scores = jnp.einsum('brhnqd,brhnkd->brhnqk', qd, kblk) * (dh ** -0.5)
    q_pos = jnp.arange(lp).reshape(nb, Q_BLOCK)
    k_pos = key_idx - half
    rel = jnp.abs(k_pos[:, None, :] - q_pos[:, :, None])
    valid = (rel <= half) & (k_pos[:, None, :] >= 0) & (k_pos[:, None, :] < L)
    alibi = -slopes[:, None, None, None] * (rel * dilation).astype(jnp.float32)
    scores = jnp.where(valid, scores + alibi[None, None], NEG_INF)
    m = jnp.max(scores, axis=-1, keepdims=True)
    e = jnp.exp(scores - m)
    den = jnp.sum(e, axis=-1, keepdims=True)
    o = jnp.einsum('brhnqk,brhnkd->brhnqd', e, vblk) / den
    lse = (m + jnp.log(den))[..., 0]

    def unstride(t):
        t = t.reshape((bsz, dilation, h, lp) + t.shape[5:])[:, :, :, :L]
        t = jnp.moveaxis(t, 3, 1)
        return t.reshape((bsz, s, h) + t.shape[4:])

    return unstride(o), unstride(lse)

def dilated_attention_mix(h, w_qkv, w_o):
    bsz, s, d = h.shape
    qkv = jnp.einsum('bsd,de->bse', h, w_qkv).astype(jnp.float32)
    qkv = qkv.reshape(bsz, s, N_GROUPS, 3, ATTN_HEADS, ATTN_HEAD_DIM)
    slopes = alibi_slopes(N_GROUPS * ATTN_HEADS).reshape(N_GROUPS, ATTN_HEADS)
    outs, lses = [], []
    for gi, (window, dil) in enumerate(ATTN_GROUPS):
        o, lse = _dilated_group(qkv[:, :, gi, 0], qkv[:, :, gi, 1], qkv[:, :, gi, 2], slopes[gi], window, dil)
        outs.append(o)
        lses.append(lse)
    o = jnp.stack(outs)
    alpha = jax.nn.softmax(jnp.stack(lses), axis=0)
    merged = jnp.sum(alpha[..., None] * o, axis=0).reshape(bsz, s, d)
    return jnp.einsum('bsd,de->bse', merged.astype(h.dtype), w_o)

def hier_moe(h, router_g, router_g_b, router_e, router_e_b, w_gate, w_up, w_down):
    bsz, s, d = h.shape
    xt = h.reshape(-1, d)
    f32 = jnp.float32
    g_logits = (xt @ router_g + router_g_b).astype(f32)
    g_prob = jax.nn.softmax(g_logits, axis=-1)
    _, g_top = lax.top_k(g_logits, 1)
    p_group = jnp.take_along_axis(g_prob, g_top, axis=-1)
    e_logits = (jnp.einsum('td,gde->tge', xt, router_e) + router_e_b).astype(f32)
    e_sel = jnp.take_along_axis(e_logits, g_top[:, :, None], axis=1)[:, 0]
    top_v, top_i = lax.top_k(e_sel, TOP_K_INNER)
    top_w = jax.nn.softmax(top_v, axis=-1) * p_group
    inner = jnp.sum(jax.nn.one_hot(top_i, EXPERTS_PER_GROUP, dtype=f32) * top_w[..., None], axis=1)
    gates = jax.nn.one_hot(g_top[:, 0], N_EXPERT_GROUPS, dtype=f32)[:, :, None] * inner[:, None, :]
    out = jnp.zeros((xt.shape[0], d), f32)
    for gi in range(N_EXPERT_GROUPS):
        hid = jax.nn.silu(jnp.einsum('td,edf->tef', xt, w_gate[gi])) * jnp.einsum('td,edf->tef', xt, w_up[gi])
        hid = hid * gates[:, gi, :, None].astype(hid.dtype)
        out = out + jnp.einsum('tef,efd->td', hid, w_down[gi]).astype(f32)
    return out.reshape(bsz, s, d).astype(h.dtype)

def first_inputs(seed: int = 0) -> dict:
    key = jax.random.key(seed)
    ks = iter(jax.random.split(key, 48))
    f32 = jnp.float32
    D, NR, NA = D_MODEL, N_RWKV_LAYERS, N_ATTN_LAYERS
    G, E, F = N_EXPERT_GROUPS, EXPERTS_PER_GROUP, D_EXPERT

    def nrm(shape, scale):
        return jax.random.normal(next(ks), shape, f32) * scale

    def uni(shape, lo, hi):
        return jax.random.uniform(next(ks), shape, f32, minval=lo, maxval=hi)

    return {
        "x": nrm((BATCH, SEQ, D), 1.0),
        "c": nrm((BATCH, D), 1.0),
        "ada_w": nrm((DEPTH, D, N_MOD * D), 0.5 * D ** -0.5),
        "ada_b": nrm((DEPTH, N_MOD * D), 0.01),
        "norm_tm_g": 1.0 + nrm((DEPTH, D), 0.02),
        "norm_cm_g": 1.0 + nrm((DEPTH, D), 0.02),
        "rw_mu": uni((NR, N_SHIFT_MIX, D), 0.0, 1.0),
        "rw_w_rkv": nrm((NR, 3, D, D), D ** -0.5),
        "rw_w0": uni((NR, N_DIRS, D), -4.5, -0.5),
        "rw_w1": nrm((NR, N_DIRS, D, D_DECAY_LORA), D ** -0.5),
        "rw_w2": nrm((NR, N_DIRS, D_DECAY_LORA, D), 0.5 * D_DECAY_LORA ** -0.5),
        "rw_a0": nrm((NR, N_DIRS, D), 0.5),
        "rw_a1": nrm((NR, N_DIRS, D, D_AAA_LORA), D ** -0.5),
        "rw_a2": nrm((NR, N_DIRS, D_AAA_LORA, D), 0.5 * D_AAA_LORA ** -0.5),
        "rw_g1": nrm((NR, N_DIRS, D, D_GATE_LORA), D ** -0.5),
        "rw_g2": nrm((NR, N_DIRS, D_GATE_LORA, D), D_GATE_LORA ** -0.5),
        "rw_k_k": 0.85 + nrm((NR, D), 0.05),
        "rw_k_a": 1.0 + nrm((NR, D), 0.05),
        "rw_r_k": nrm((NR, RWKV_HEADS, RWKV_HEAD), 0.1),
        "rw_ln_w": 1.0 + nrm((NR, D), 0.02),
        "rw_ln_b": nrm((NR, D), 0.01),
        "rw_w_o": nrm((NR, D, D), D ** -0.5),
        "at_w_qkv": nrm((NA, D, QKV_WIDTH), D ** -0.5),
        "at_w_o": nrm((NA, D, D), D ** -0.5),
        "moe_router_g": nrm((DEPTH, D, G), D ** -0.5),
        "moe_router_g_b": nrm((DEPTH, G), 0.01),
        "moe_router_e": nrm((DEPTH, G, D, E), D ** -0.5),
        "moe_router_e_b": nrm((DEPTH, G, E), 0.01),
        "moe_w_gate": nrm((DEPTH, G, E, D, F), D ** -0.5),
        "moe_w_up": nrm((DEPTH, G, E, D, F), D ** -0.5),
        "moe_w_down": nrm((DEPTH, G, E, F, D), F ** -0.5),
        "final_g": 1.0 + nrm((D,), 0.02),
    }

def first_block(x, c, ada_w, ada_b, norm_tm_g, norm_cm_g,
              rw_mu, rw_w_rkv, rw_w0, rw_w1, rw_w2, rw_a0, rw_a1, rw_a2, rw_g1, rw_g2,
              rw_k_k, rw_k_a, rw_r_k, rw_ln_w, rw_ln_b, rw_w_o,
              at_w_qkv, at_w_o,
              moe_router_g, moe_router_g_b, moe_router_e, moe_router_e_b,
              moe_w_gate, moe_w_up, moe_w_down, final_g):
    silu_c = jax.nn.silu(c)
    for i in range(DEPTH):
        mod = silu_c @ ada_w[i] + ada_b[i]
        sh_t, sc_t, ga_t, sh_c, sc_c, ga_c = jnp.split(mod, N_MOD, axis=-1)
        hn = modulate(rms_norm(x, norm_tm_g[i]), sh_t, sc_t)
        j = i // N_MIXERS
        if i % N_MIXERS == 0:
            tm = rwkv7_mix(hn, rw_mu[j], rw_w_rkv[j], rw_w0[j], rw_w1[j], rw_w2[j],
                           rw_a0[j], rw_a1[j], rw_a2[j], rw_g1[j], rw_g2[j],
                           rw_k_k[j], rw_k_a[j], rw_r_k[j], rw_ln_w[j], rw_ln_b[j], rw_w_o[j])
        else:
            tm = dilated_attention_mix(hn, at_w_qkv[j], at_w_o[j])
        x = x + ga_t[:, None, :] * tm
        hn = modulate(rms_norm(x, norm_cm_g[i]), sh_c, sc_c)
        cm = hier_moe(hn, moe_router_g[i], moe_router_g_b[i], moe_router_e[i], moe_router_e_b[i],
                      moe_w_gate[i], moe_w_up[i], moe_w_down[i])
        x = x + ga_c[:, None, :] * cm
    return rms_norm(x, final_g)


DEPTH_2 = 4

N_MIXERS_2 = 4
N_HEADS = 8
HEAD_DIM = D_MODEL // N_HEADS
D_FF = 4 * D_MODEL
ROPE_THETA = 10000.0
NORM_EPS = 1e-6
NEG_INF_2 = -1e30

NSA_KV_GROUPS = 2
NSA_HEADS_PER_GROUP = N_HEADS // NSA_KV_GROUPS
NSA_CMP_BLOCK = 32
NSA_CMP_STRIDE = 16
NSA_SEL_BLOCK = 64
NSA_SEL_TOPK = 16
NSA_WINDOW = 512
NSA_QBLOCK = 64
NSA_FORCE_BONUS = 1000.0
NSA_IN_DIM = N_HEADS * HEAD_DIM + 6 * NSA_KV_GROUPS * HEAD_DIM + 3 * N_HEADS

SB_QBLOCK = 128

CONV_WIDTH = 31

MOBA_BLOCK = 256
MOBA_TOPK = 3
MOBA_QBLOCK = 32

N_NSA = (DEPTH_2 + 3) // 4
N_SB = (DEPTH_2 + 2) // 4
N_CONV = (DEPTH_2 + 1) // 4
N_MOBA = DEPTH_2 // 4


def _rms_norm(x, g):
    xf = x.astype(jnp.float32)
    y = xf * lax.rsqrt(jnp.mean(xf * xf, axis=-1, keepdims=True) + NORM_EPS)
    return (y * g.astype(jnp.float32)).astype(x.dtype)

def _rope_tables(seq):
    half = HEAD_DIM // 2
    inv_freq = ROPE_THETA ** (-jnp.arange(half, dtype=jnp.float32) / half)
    ang = jnp.arange(seq, dtype=jnp.float32)[:, None] * inv_freq[None, :]
    return jnp.cos(ang), jnp.sin(ang)

def _apply_rope(x, cos, sin):
    xf = x.astype(jnp.float32)
    x1, x2 = jnp.split(xf, 2, axis=-1)
    c = cos[None, :, None, :]
    s = sin[None, :, None, :]
    return jnp.concatenate([x1 * c - x2 * s, x1 * s + x2 * c], axis=-1).astype(x.dtype)

def _masked_softmax(logits, mask):
    z = jnp.where(mask, logits.astype(jnp.float32), NEG_INF_2)
    return jnp.where(mask, jax.nn.softmax(z, axis=-1), 0.0)

def _nsa_mixer(h, w_in, q_gain, k_gain, cmp_pos, w_cmp, w_out, cos, sin):
    B, S, _ = h.shape
    H, G, HG, DH = N_HEADS, NSA_KV_GROUPS, NSA_HEADS_PER_GROUP, HEAD_DIM
    L, STR, SB, W, QB = NSA_CMP_BLOCK, NSA_CMP_STRIDE, NSA_SEL_BLOCK, NSA_WINDOW, NSA_QBLOCK
    sizes = [H * DH] + [G * DH] * 6
    q, kc, vc, ks, vs, kw, vw, gates = jnp.split(h @ w_in, np.cumsum(sizes).tolist(), axis=-1)
    q = _apply_rope(_rms_norm(q.reshape(B, S, H, DH), q_gain), cos, sin)
    kc, ks, kw = [_apply_rope(_rms_norm(k.reshape(B, S, G, DH), k_gain[i]), cos, sin)
                  for i, k in enumerate((kc, ks, kw))]
    vc, vs, vw = [v.reshape(B, S, G, DH) for v in (vc, vs, vw)]
    gates = jax.nn.sigmoid(gates.astype(jnp.float32)).reshape(B, S, 3, G, HG)
    n_cmp = (S - L) // STR + 1
    cmp_start = jnp.arange(n_cmp) * STR
    cidx = cmp_start[:, None] + jnp.arange(L)[None, :]
    kc = jnp.einsum('bnlgd,lde->bnge', kc[:, cidx] + cmp_pos[0][None, None, :, None, :], w_cmp[0])
    vc = jnp.einsum('bnlgd,lde->bnge', vc[:, cidx] + cmp_pos[1][None, None, :, None, :], w_cmp[1])
    cmp_end = cmp_start + L - 1
    n_sel = S // SB
    sel_start = jnp.arange(n_sel) * SB
    overlap = ((cmp_start[:, None] < sel_start[None, :] + SB)
               & (cmp_start[:, None] + L > sel_start[None, :])).astype(jnp.float32)
    topk = min(NSA_SEL_TOPK, n_sel)
    ks_blk = ks.reshape(B, n_sel, SB, G, DH).transpose(0, 3, 1, 2, 4)
    vs_blk = vs.reshape(B, n_sel, SB, G, DH).transpose(0, 3, 1, 2, 4)
    kw_pad = jnp.pad(kw, ((0, 0), (W, 0), (0, 0), (0, 0)))
    vw_pad = jnp.pad(vw, ((0, 0), (W, 0), (0, 0), (0, 0)))
    scale = DH ** -0.5
    b_ix = jnp.arange(B)[:, None, None, None]
    g_ix = jnp.arange(G)[None, None, :, None]
    blk = jnp.arange(n_sel)
    in_blk = jnp.arange(SB)
    win_off = jnp.arange(W + QB) - W

    def chunk(c0):
        t = c0 + jnp.arange(QB)
        qc = lax.dynamic_slice_in_dim(q, c0, QB, axis=1).reshape(B, QB, G, HG, DH)
        p_c = _masked_softmax(jnp.einsum('bqghd,bngd->bqghn', qc, kc) * scale,
                              (cmp_end[None, :] <= t[:, None])[None, :, None, None, :])
        o_c = jnp.einsum('bqghn,bngd->bqghd', p_c.astype(vc.dtype), vc)
        imp = jnp.einsum('bqgn,nj->bqgj', p_c.sum(axis=3), overlap)
        cur = c0 // SB
        forced = (blk == 0) | (blk == cur) | (blk == cur - 1)
        imp = jnp.where(blk <= cur, imp + NSA_FORCE_BONUS * forced, -1.0)
        _, idx = lax.top_k(imp, topk)
        k_sel = ks_blk[b_ix, g_ix, idx].reshape(B, QB, G, topk * SB, DH)
        v_sel = vs_blk[b_ix, g_ix, idx].reshape(B, QB, G, topk * SB, DH)
        pos = (idx[..., None] * SB + in_blk).reshape(B, QB, G, 1, topk * SB)
        p_s = _masked_softmax(jnp.einsum('bqghd,bqgmd->bqghm', qc, k_sel) * scale,
                              pos <= t[None, :, None, None, None])
        o_s = jnp.einsum('bqghm,bqgmd->bqghd', p_s.astype(v_sel.dtype), v_sel)
        pos_w = c0 + win_off
        diff = t[:, None] - pos_w[None, :]
        m_w = ((pos_w[None, :] >= 0) & (diff >= 0) & (diff < W))[None, :, None, None, :]
        kwc = lax.dynamic_slice_in_dim(kw_pad, c0, W + QB, axis=1)
        vwc = lax.dynamic_slice_in_dim(vw_pad, c0, W + QB, axis=1)
        p_w = _masked_softmax(jnp.einsum('bqghd,bkgd->bqghk', qc, kwc) * scale, m_w)
        o_w = jnp.einsum('bqghk,bkgd->bqghd', p_w.astype(vwc.dtype), vwc)
        g = lax.dynamic_slice_in_dim(gates, c0, QB, axis=1)[..., None]
        o = g[:, :, 0] * o_c + g[:, :, 1] * o_s + g[:, :, 2] * o_w
        return o.reshape(B, QB, H * DH).astype(h.dtype)

    out = lax.map(chunk, jnp.arange(S // QB) * QB)
    out = jnp.transpose(out, (1, 0, 2, 3)).reshape(B, S, H * DH)
    return out @ w_out

def _stick_breaking_mixer(h, w_in, w_out):
    B, S, _ = h.shape
    H, DH, QB = N_HEADS, HEAD_DIM, SB_QBLOCK
    q, k, v = [a.reshape(B, S, H, DH) for a in jnp.split(h @ w_in, 3, axis=-1)]
    scale = DH ** -0.5
    s_idx = jnp.arange(S)

    def chunk(c0):
        t = c0 + jnp.arange(QB)
        qc = lax.dynamic_slice_in_dim(q, c0, QB, axis=1)
        z = jnp.einsum('bqhd,bshd->bhqs', qc, k).astype(jnp.float32) * scale
        mask = (s_idx[None, :] < t[:, None])[None, None]
        log_beta = jax.nn.log_sigmoid(z)
        log_one_minus = jnp.where(mask, jax.nn.log_sigmoid(-z), 0.0)
        between = lax.cumsum(log_one_minus, axis=3, reverse=True) - log_one_minus
        a = jnp.where(mask, jnp.exp(log_beta + between), 0.0)
        o = jnp.einsum('bhqs,bshd->bqhd', a.astype(v.dtype), v)
        return o.reshape(B, QB, H * DH)

    out = lax.map(chunk, jnp.arange(S // QB) * QB)
    out = jnp.transpose(out, (1, 0, 2, 3)).reshape(B, S, H * DH)
    return out @ w_out

def _conformer_conv_mixer(h, w_in, dw_w, dw_b, ln_g, ln_b, w_out):
    a, b = jnp.split(h @ w_in, 2, axis=-1)
    u = a * jax.nn.sigmoid(b)
    u = lax.conv_general_dilated(u, dw_w[:, None, :], window_strides=(1,),
                                 padding=[(CONV_WIDTH - 1, 0)],
                                 dimension_numbers=('NWC', 'WIO', 'NWC'),
                                 feature_group_count=D_MODEL) + dw_b
    uf = u.astype(jnp.float32)
    mu = jnp.mean(uf, axis=-1, keepdims=True)
    var = jnp.mean(jnp.square(uf - mu), axis=-1, keepdims=True)
    un = (uf - mu) * lax.rsqrt(var + NORM_EPS) * ln_g.astype(jnp.float32) + ln_b.astype(jnp.float32)
    return jax.nn.silu(un).astype(h.dtype) @ w_out

def _moba_mixer(h, w_in, q_gain, k_gain, w_out, cos, sin):
    B, S, _ = h.shape
    H, DH, BS, QB = N_HEADS, HEAD_DIM, MOBA_BLOCK, MOBA_QBLOCK
    q, k, v = [a.reshape(B, S, H, DH) for a in jnp.split(h @ w_in, 3, axis=-1)]
    q = _apply_rope(_rms_norm(q, q_gain), cos, sin)
    k = _apply_rope(_rms_norm(k, k_gain), cos, sin)
    n_blk = -(-S // BS)
    pad = n_blk * BS - S
    kp = jnp.pad(k, ((0, 0), (0, pad), (0, 0), (0, 0)))
    vp = jnp.pad(v, ((0, 0), (0, pad), (0, 0), (0, 0)))
    k_blocks = kp.reshape(B, n_blk, BS, H, DH)
    k_mean = jnp.mean(k_blocks.astype(jnp.float32), axis=2)
    kb_t = k_blocks.transpose(0, 3, 1, 2, 4)
    vb_t = vp.reshape(B, n_blk, BS, H, DH).transpose(0, 3, 1, 2, 4)
    topk = min(MOBA_TOPK, n_blk)
    scale = DH ** -0.5
    b_ix = jnp.arange(B)[:, None, None, None]
    h_ix = jnp.arange(H)[None, None, :, None]
    blk = jnp.arange(n_blk)

    def chunk(c0):
        t = c0 + jnp.arange(QB)
        qc = lax.dynamic_slice_in_dim(q, c0, QB, axis=1)
        cur = c0 // BS
        gate = jnp.einsum('bqhd,bnhd->bqhn', qc.astype(jnp.float32), k_mean)
        gate = jnp.where(blk < cur, gate, NEG_INF_2)
        _, idx = lax.top_k(gate, topk)
        valid = idx < cur
        k_sel = kb_t[b_ix, h_ix, idx].reshape(B, QB, H, topk * BS, DH)
        v_sel = vb_t[b_ix, h_ix, idx].reshape(B, QB, H, topk * BS, DH)
        s_past = jnp.einsum('bqhd,bqhmd->bqhm', qc, k_sel) * scale
        m_past = jnp.broadcast_to(valid[..., None], (B, QB, H, topk, BS)).reshape(B, QB, H, topk * BS)
        own0 = cur * BS
        k_own = lax.dynamic_slice_in_dim(kp, own0, BS, axis=1)
        v_own = lax.dynamic_slice_in_dim(vp, own0, BS, axis=1)
        s_own = jnp.einsum('bqhd,bkhd->bqhk', qc, k_own) * scale
        m_own = jnp.broadcast_to(((own0 + jnp.arange(BS))[None, :] <= t[:, None])[None, :, None, :],
                                 (B, QB, H, BS))
        p = _masked_softmax(jnp.concatenate([s_past, s_own], axis=-1),
                            jnp.concatenate([m_past, m_own], axis=-1))
        p = p.astype(v.dtype)
        o = (jnp.einsum('bqhm,bqhmd->bqhd', p[..., :topk * BS], v_sel)
             + jnp.einsum('bqhk,bkhd->bqhd', p[..., topk * BS:], v_own))
        return o.reshape(B, QB, H * DH)

    out = lax.map(chunk, jnp.arange(S // QB) * QB)
    out = jnp.transpose(out, (1, 0, 2, 3)).reshape(B, S, H * DH)
    return out @ w_out

def second_inputs(seed: int = 0) -> dict:
    key = jax.random.key(seed)
    keys = iter(jax.random.split(key, 32))

    def w(shape, fan_in):
        return jax.random.normal(next(keys), shape, jnp.float32) * (fan_in ** -0.5)

    def gain(shape):
        return 1.0 + 0.05 * jax.random.normal(next(keys), shape, jnp.float32)

    def small(shape, s):
        return s * jax.random.normal(next(keys), shape, jnp.float32)

    D, DH, L = D_MODEL, HEAD_DIM, NSA_CMP_BLOCK
    return {
        'x': jax.random.normal(next(keys), (BATCH, SEQ, D), jnp.float32),
        'attn_norm': gain((DEPTH_2, D)),
        'mlp_norm': gain((DEPTH_2, D)),
        'mlp_w_up': w((DEPTH_2, D, D_FF), D),
        'mlp_w_down': w((DEPTH_2, D_FF, D), D_FF),
        'nsa_w_in': w((N_NSA, D, NSA_IN_DIM), D),
        'nsa_q_norm': gain((N_NSA, DH)),
        'nsa_k_norm': gain((N_NSA, 3, DH)),
        'nsa_cmp_pos': small((N_NSA, 2, L, DH), 0.1),
        'nsa_w_cmp': w((N_NSA, 2, L, DH, DH), L * DH),
        'nsa_w_out': w((N_NSA, N_HEADS * DH, D), N_HEADS * DH),
        'sb_w_in': w((N_SB, D, 3 * N_HEADS * DH), D),
        'sb_w_out': w((N_SB, N_HEADS * DH, D), N_HEADS * DH),
        'conv_w_in': w((N_CONV, D, 2 * D), D),
        'conv_dw_w': w((N_CONV, CONV_WIDTH, D), CONV_WIDTH),
        'conv_dw_b': small((N_CONV, D), 0.02),
        'conv_ln_g': gain((N_CONV, D)),
        'conv_ln_b': small((N_CONV, D), 0.02),
        'conv_w_out': w((N_CONV, D, D), D),
        'moba_w_in': w((N_MOBA, D, 3 * N_HEADS * DH), D),
        'moba_q_norm': gain((N_MOBA, DH)),
        'moba_k_norm': gain((N_MOBA, DH)),
        'moba_w_out': w((N_MOBA, N_HEADS * DH, D), N_HEADS * DH),
    }

def second_block(x, attn_norm, mlp_norm, mlp_w_up, mlp_w_down,
              nsa_w_in, nsa_q_norm, nsa_k_norm, nsa_cmp_pos, nsa_w_cmp, nsa_w_out,
              sb_w_in, sb_w_out,
              conv_w_in, conv_dw_w, conv_dw_b, conv_ln_g, conv_ln_b, conv_w_out,
              moba_w_in, moba_q_norm, moba_k_norm, moba_w_out):
    cos, sin = _rope_tables(x.shape[1])
    for i in range(DEPTH_2):
        m, j = i % N_MIXERS_2, i // N_MIXERS_2
        h = _rms_norm(x, attn_norm[i])
        if m == 0:
            y = _nsa_mixer(h, nsa_w_in[j], nsa_q_norm[j], nsa_k_norm[j], nsa_cmp_pos[j],
                           nsa_w_cmp[j], nsa_w_out[j], cos, sin)
        elif m == 1:
            y = _stick_breaking_mixer(h, sb_w_in[j], sb_w_out[j])
        elif m == 2:
            y = _conformer_conv_mixer(h, conv_w_in[j], conv_dw_w[j], conv_dw_b[j],
                                      conv_ln_g[j], conv_ln_b[j], conv_w_out[j])
        else:
            y = _moba_mixer(h, moba_w_in[j], moba_q_norm[j], moba_k_norm[j], moba_w_out[j], cos, sin)
        x = x + y.astype(x.dtype)
        hm = _rms_norm(x, mlp_norm[i])
        x = x + jnp.square(jax.nn.relu(hm @ mlp_w_up[i])) @ mlp_w_down[i]
    return x


def setup_inputs(seed=0):
    out = dict(first_inputs(seed))
    for name, value in second_inputs(seed + 1).items():
        if name != "x":
            out[name + "_2"] = value
    return out


def reference(
    x, c, ada_w, ada_b, norm_tm_g, norm_cm_g, rw_mu, rw_w_rkv, rw_w0, rw_w1, rw_w2, rw_a0,
    rw_a1, rw_a2, rw_g1, rw_g2, rw_k_k, rw_k_a, rw_r_k, rw_ln_w, rw_ln_b, rw_w_o, at_w_qkv,
    at_w_o, moe_router_g, moe_router_g_b, moe_router_e, moe_router_e_b, moe_w_gate, moe_w_up,
    moe_w_down, final_g, attn_norm_2, mlp_norm_2, mlp_w_up_2, mlp_w_down_2, nsa_w_in_2,
    nsa_q_norm_2, nsa_k_norm_2, nsa_cmp_pos_2, nsa_w_cmp_2, nsa_w_out_2, sb_w_in_2, sb_w_out_2,
    conv_w_in_2, conv_dw_w_2, conv_dw_b_2, conv_ln_g_2, conv_ln_b_2, conv_w_out_2, moba_w_in_2,
    moba_q_norm_2, moba_k_norm_2, moba_w_out_2,
):
    x = first_block(
        x, c, ada_w, ada_b, norm_tm_g, norm_cm_g, rw_mu, rw_w_rkv, rw_w0, rw_w1, rw_w2, rw_a0,
        rw_a1, rw_a2, rw_g1, rw_g2, rw_k_k, rw_k_a, rw_r_k, rw_ln_w, rw_ln_b, rw_w_o, at_w_qkv,
        at_w_o, moe_router_g, moe_router_g_b, moe_router_e, moe_router_e_b, moe_w_gate,
        moe_w_up, moe_w_down, final_g,
    )
    return second_block(
        x, attn_norm_2, mlp_norm_2, mlp_w_up_2, mlp_w_down_2, nsa_w_in_2, nsa_q_norm_2,
        nsa_k_norm_2, nsa_cmp_pos_2, nsa_w_cmp_2, nsa_w_out_2, sb_w_in_2, sb_w_out_2,
        conv_w_in_2, conv_dw_w_2, conv_dw_b_2, conv_ln_g_2, conv_ln_b_2, conv_w_out_2,
        moba_w_in_2, moba_q_norm_2, moba_k_norm_2, moba_w_out_2,
    )


_drawn_inputs = setup_inputs


def setup_inputs(seed=0):
    import zlib

    import numpy as np

    out = dict(_drawn_inputs(seed))
    spreads = {}
    factors = {'norm_tm_g': 3.721,
     'rw_ln_w': 6.16,
     'rw_ln_b': 8.0,
     'moe_router_g_b': 3.836,
     'moe_router_e_b': 4.243,
     'nsa_q_norm_2': 4.232,
     'nsa_k_norm_2': 4.683,
     'conv_dw_b_2': 4.297,
     'conv_ln_g_2': 3.104,
     'conv_ln_b_2': 8.0,
     'moba_q_norm_2': 8.0,
     'moba_k_norm_2': 8.0}
    for name, (base, spread) in spreads.items():
        noise = np.random.default_rng([zlib.crc32(name.encode()), seed]).standard_normal(out[name].shape)
        drawn = base * np.exp(spread * noise) if base else spread * noise
        out[name] = __import__('jax').numpy.asarray(drawn.astype(out[name].dtype))
    for name, factor in factors.items():
        out[name] = (out[name] * factor).astype(out[name].dtype)
    return out
```

```python
from contextlib import ExitStack

import numpy as np

import concourse.bass as bass
from concourse import mybir

F32 = mybir.dt.float32
F32R = mybir.dt.float32r
ALU = mybir.AluOpType
ACT = mybir.ActivationFunctionType
AX_X = mybir.AxisListType.X

P = 128
S = 256
D = 1024
C = D // P
RING = 4
PREP = 2
BLK = 2048
EPS = 1e-6
GN_EPS = 64e-5
EXPERTS = 32
UNITS = 16
NEG = -1e30
HEADS = 8
DH = 128
DILATIONS = (1, 4, 16)
CONV_W = 31
N_CMP = 15
HALF_LOG = 0.6065306597126334

COLS = {}


def _columns():
    at = 0
    for name, n in (
        [("c", C)] + [(f"norm_tm{i}", C) for i in range(2)] + [(f"norm_cm{i}", C) for i in range(2)]
        + [("final", C)] + [(f"attn_norm{i}", C) for i in range(4)] + [(f"mlp_norm{i}", C) for i in range(4)]
        + [("mu", 6 * C), ("w0", 2 * C), ("a0", 2 * C), ("kk", C), ("ka", C), ("rk", C), ("lnw", C), ("lnb", C)]
        + [("ada_b0", 6 * C), ("ada_b1", 6 * C), ("dw_b", C), ("cln_g", C), ("cln_b", C)]
        + [("nsa_q", 1), ("nsa_k", 3), ("moba_q", 1), ("moba_k", 1)]
        + [("dw_w", CONV_W * C), ("cmp_pos", 2 * 32)]
        + [("router0", C * 36), ("router1", C * 36), ("nsa_gate", C * 24)]
    ):
        COLS[name] = (at, n)
        at += n
    return at


NCOLS = _columns()

ADA = 24 * 2
ORDER = [("rkv", 12), ("lora", 2), ("rwo", 4), ("moe0", 3 * EXPERTS), ("dilA", 18), ("dilB", 18), ("dilo", 4),
         ("moe1", 3 * EXPERTS), ("nsa", 10), ("nsao", 4), ("mlp0", 2 * UNITS), ("sb", 12), ("sbo", 4),
         ("mlp1", 2 * UNITS), ("conv", 8), ("convo", 4), ("mlp2", 2 * UNITS), ("moba", 12), ("mobao", 4),
         ("mlp3", 2 * UNITS)]
Q0 = {}
_n = 0
for _name, _k in ORDER:
    Q0[_name] = _n
    _n += _k
NSPLIT = _n
NBLK = ADA + NSPLIT


def arrange(I):
    f = np.float32
    g = {k: np.asarray(v) for k, v in I.items()}

    def up(w):
        n = w.shape[1] // 256
        return w.reshape(C, P, n, 256).transpose(2, 1, 0, 3).reshape(n, P, BLK)

    def down(w):
        n = w.shape[0] // 256
        return w.reshape(n, 2, P, D).transpose(0, 2, 1, 3).reshape(n, P, BLK)

    def lagged(ups, downs):
        parts = [ups[0]]
        for e in range(len(downs)):
            if e + 1 < len(ups):
                parts.append(ups[e + 1])
            parts.append(downs[e])
        return parts

    def experts(i):
        G, U, Dn = (g[k][i].reshape((EXPERTS,) + g[k].shape[3:]) for k in ("moe_w_gate", "moe_w_up", "moe_w_down"))
        return lagged([np.concatenate([up(G[e]), up(U[e])]) for e in range(EXPERTS)], [down(Dn[e]) for e in range(EXPERTS)])

    def mlp(i):
        u, d = up(g["mlp_w_up_2"][i]), down(g["mlp_w_down_2"][i])
        return lagged([u[j:j + 1] for j in range(UNITS)], [d[j:j + 1] for j in range(UNITS)])

    qkv = g["at_w_qkv"][0].reshape(D, 3, 3, 4, 256)
    dil = []
    for half in range(2):
        for gi in range(3):
            for part in range(3):
                for pr in range(2):
                    dil.append(up(qkv[:, gi, part, 2 * half + pr]))
    conv = g["conv_w_in_2"][0].reshape(D, 2, 4, 256)
    lora = [np.concatenate([g["rw_w1"][0, 0], g["rw_w1"][0, 1], g["rw_a1"][0, 0], g["rw_a1"][0, 1]], 1),
            np.concatenate([g["rw_g1"][0, 0], g["rw_g1"][0, 1]], 1)]
    parts = [up(g["ada_w"][0]), up(g["ada_w"][1])]
    parts += [up(g["rw_w_rkv"][0, j]) for j in range(3)] + [up(w) for w in lora] + [up(g["rw_w_o"][0])]
    parts += experts(0) + dil + [up(g["at_w_o"][0])] + experts(1)
    parts += [up(g["nsa_w_in_2"][0][:, :2560]), up(g["nsa_w_out_2"][0])] + mlp(0)
    parts += [up(g["sb_w_in_2"][0]), up(g["sb_w_out_2"][0])] + mlp(1)
    parts += [up(conv[:, b, j]) for j in range(4) for b in (1, 0)] + [up(g["conv_w_out_2"][0])] + mlp(2)
    parts += [up(g["moba_w_in_2"][0]), up(g["moba_w_out_2"][0])] + mlp(3)
    stream = np.concatenate(parts)
    assert stream.shape == (NBLK, P, BLK)

    def col(v):
        return v.reshape(-1, P).T

    cols = np.zeros((P, NCOLS), f)

    def put(name, a):
        at, n = COLS[name]
        cols[:, at:at + n] = a.reshape(P, n)

    put("c", col(g["c"]))
    for i in range(2):
        put(f"norm_tm{i}", col(g["norm_tm_g"][i]))
        put(f"norm_cm{i}", col(g["norm_cm_g"][i]))
        put(f"ada_b{i}", col(g["ada_b"][i]))
        router = np.concatenate([g["moe_router_g"][i], g["moe_router_e"][i].transpose(1, 0, 2).reshape(D, EXPERTS)], 1)
        put(f"router{i}", router.reshape(C, P, 36).transpose(1, 0, 2))
    put("final", col(g["final_g"]))
    for i in range(4):
        put(f"attn_norm{i}", col(g["attn_norm_2"][i]))
        put(f"mlp_norm{i}", col(g["mlp_norm_2"][i]))
    for name, k in (("mu", "rw_mu"), ("w0", "rw_w0"), ("a0", "rw_a0"), ("kk", "rw_k_k"), ("ka", "rw_k_a"), ("rk", "rw_r_k"),
                    ("lnw", "rw_ln_w"), ("lnb", "rw_ln_b"), ("dw_b", "conv_dw_b_2"), ("cln_g", "conv_ln_g_2"),
                    ("cln_b", "conv_ln_b_2"), ("nsa_q", "nsa_q_norm_2"), ("nsa_k", "nsa_k_norm_2"),
                    ("moba_q", "moba_q_norm_2"), ("moba_k", "moba_k_norm_2"), ("dw_w", "conv_dw_w_2"),
                    ("cmp_pos", "nsa_cmp_pos_2")):
        put(name, col(g[k][0]))
    put("nsa_gate", g["nsa_w_in_2"][0][:, 2560:].reshape(C, P, 24).transpose(1, 0, 2))
    rows = np.zeros((1, 72), f)
    for i in range(2):
        rows[0, 36 * i:36 * i + 4] = g["moe_router_g_b"][i]
        rows[0, 36 * i + 4:36 * i + 36] = g["moe_router_e_b"][i].reshape(-1)
    lora2 = np.concatenate([g["rw_w2"][0].reshape(P, D), g["rw_a2"][0].reshape(P, D),
                            g["rw_g2"][0].transpose(1, 0, 2).reshape(P, 2 * D)], 1)
    wcmp = g["nsa_w_cmp_2"][0].transpose(2, 0, 1, 3).reshape(P, 2 * 32 * DH)
    xT = g["x"][0].T.reshape(C, P, S).transpose(1, 0, 2).reshape(P, C * S)
    return {"stream": stream, "cols": cols, "rows": rows, "lora2": np.ascontiguousarray(lora2),
            "wcmp": np.ascontiguousarray(wcmp), "xT": np.ascontiguousarray(xT)}


def constants():
    f = np.float32
    i = np.arange(P)
    r, c = i[:, None], i[None, :]
    mats = {"ident": (r == c), "ones": np.ones((P, P)), "blk64": (r // 64 == c // 64)}
    rot = np.zeros((P, P))
    rot[i[:64] + 64, i[:64]] = -1.0
    rot[i[:64], i[:64] + 64] = 1.0
    mats["rot"] = rot
    rw = {}
    for lev in range(7):
        b = 1 << lev
        low = (r // (2 * b) == c // (2 * b)) & (r // b % 2 == 1) & (c // b % 2 == 0)
        rw[f"low{lev}"], rw[f"up{lev}"] = low, low.T
    rw["ui"], rw["us"], rw["li"], rw["ls"] = (r <= c), (r < c), (r >= c), (r > c)
    tok = np.arange(S)
    q = (np.arange(2)[None, :, None] * P + i[:, None, None])
    k = tok[None, None, :]
    at = {"causal": np.where(k <= q, 0.0, NEG), "strictadd": np.where(k < q, 0.0, NEG), "strict": (k < q),
          "dist": np.abs(k - q)}
    for n, dil in enumerate(DILATIONS):
        window = (128, 512, 2048)[n]
        ok = ((k - q) % dil == 0) & (np.abs(k - q) // dil <= window // (2 * dil))
        at[f"dil{n}"] = np.where(ok, 0.0, NEG)
    n = 16 * np.arange(16)[None, None, :] + 31
    cm = (n <= q) & (np.arange(16)[None, None, :] < N_CMP)
    at["cmpadd"], at["cmpmul"] = np.where(cm, 0.0, NEG), cm
    half = DH // 2
    inv = (10000.0 ** (-np.arange(half, dtype=f) / f(half))).astype(f)
    ang = (tok.astype(f)[None, :] * inv[:, None]).astype(f)
    at["cos"] = np.concatenate([np.cos(ang)] * 2)
    at["sin"] = np.concatenate([np.sin(ang)] * 2)

    def pack(d):
        where, at_, out = {}, 0, []
        for name, a in d.items():
            a = np.asarray(a, f).reshape(P, -1)
            where[name] = (at_, a.shape[1])
            at_ += a.shape[1]
            out.append(a)
        return where, np.ascontiguousarray(np.concatenate(out, 1))

    return pack(mats), pack(rw), pack(at)


(MATS, MATS_A), (RWM, RWM_A), (ATM, ATM_A) = constants()


def slopes():
    n = 3 * HEADS
    return [2.0 ** (-8.0 * (j + 1) / n) for j in range(n)]


NORMS = ["tm0", "cm0", "tm1", "cm1", "final", "at0", "ml0", "at1", "ml1", "at2", "ml2", "at3", "ml3"]
GAIN = {"tm0": None, "cm0": None, "tm1": None, "cm1": None, "final": "final", "at0": "attn_norm0", "ml0": "mlp_norm0",
        "at1": "attn_norm1", "ml1": "mlp_norm1", "at2": "attn_norm2", "ml2": "mlp_norm2", "at3": "attn_norm3",
        "ml3": "mlp_norm3"}
VERSIONS = ["mix0", "mix1", "mix2", "mix3", "mix4", "mix5", "rwo", "moe0", "dil", "dilo", "moe1", "nsa", "nsao", "mlp0",
            "sb", "sbo", "mlp1", "conv", "convo", "mlp2", "moba", "mobao", "mlp3"]
VER = {n: i for i, n in enumerate(VERSIONS)}
SLOPES = slopes()
RW_LEVELS = 5
SOFT = {"nsa": dict(jobs=16, lo=4), "dilA": dict(jobs=8, lo=4), "dilB": dict(jobs=8, lo=4), "moba": dict(jobs=16, lo=2),
        "sb": dict(jobs=16, lo=2)}

LO, HI, SKIP = {}, {}, {}
_c = {"lo": 0, "hi": 0}


def _plan(name, lo, hi=0, align=False):
    SKIP[name] = -_c["lo"] % 4 if align else 0
    _c["lo"] += SKIP[name]
    LO[name], HI[name] = _c["lo"], _c["hi"]
    _c["lo"] += lo
    _c["hi"] += hi


RW_TILES = 2 + 2 * (1 + 6) + 2 * (3 * RW_LEVELS - 1) + 2 + 2 * 9 + 6
_plan("ada", 1)
_plan("norm_tm0", 1)
_plan("rkv", 12)
_plan("lora", 3)
_plan("rwkv", C * RW_TILES, C * 4)
_plan("rwo", 4)


def _plan_moe(i):
    _plan(f"norm_cm{i}", 1)
    _plan(f"route{i}", 1)
    _plan(f"gate{i}", 16)
    _plan(f"moe{i}", 2 * EXPERTS, 4, align=True)


def _plan_mlp(i):
    _plan(f"norm_ml{i}", 1)
    _plan(f"mlp{i}", UNITS, 4, align=True)


_plan_moe(0)
_plan("norm_tm1", 1)
for _h in "AB":
    _plan(f"dil{_h}", 18)
    _plan(f"att_dil{_h}", 8 * 4, 4)
_plan("dilo", 4)
_plan_moe(1)
_plan("norm_final", 1)
_plan("norm_at0", 1)
_plan("nsa", 10)
_plan("nsagate", 1)
_plan("nsapost", 2 * 7)
_plan("nsacmp", 1, 1)
_plan("att_nsa", 16 * 4, 8)
_plan("nsao", 4)
_plan_mlp(0)
_plan("norm_at1", 1)
_plan("sb", 12)
_plan("att_sb", 16 * 2, 8)
_plan("sbo", 4)
_plan_mlp(1)
_plan("norm_at2", 1)
_plan("conv", 8)
_plan("convn", 2)
_plan("convo", 4)
_plan_mlp(2)
_plan("norm_at3", 1)
_plan("moba", 12)
_plan("mobapost", 2 * 8)
_plan("att_moba", 16 * 2, 8)
_plan("mobao", 4)
_plan_mlp(3)

DONE = {}
LAST_READ = {}
DOWN0 = {}
_d = 0
for _name, _k in ORDER:
    q = Q0[_name]
    if _name.startswith(("moe", "mlp")):
        ups, n = (2, EXPERTS) if _name[:3] == "moe" else (1, UNITS)
        DOWN0[_name] = _d
        for u in range(ups):
            DONE[q + u] = ("lo", LO[_name] + u + 1)
        for e in range(n):
            b = q + ups + e * (ups + 1)
            if e + 1 < n:
                for u in range(ups):
                    DONE[b + u] = ("lo", LO[_name] + ups * (e + 1) + u + 1)
                DONE[b + ups] = ("down", _d + e + 1)
            else:
                DONE[b] = ("down", _d + e + 1)
        LAST_READ[_name] = ("lo", LO[_name] + ups * n)
        _d += n
    elif _name == "lora":
        DONE[q], DONE[q + 1] = ("lo", LO["lora"] + 2), ("lo", LO["lora"] + 3)
    else:
        for j in range(_k):
            DONE[q + j] = ("lo", LO[_name] + j + 1)
        LAST_READ[_name] = ("lo", LO[_name] + _k)
for j in range(3):
    LAST_READ[f"mix{j}"] = ("lo", LO["rkv"] + 4 * (j + 1))
    LAST_READ[f"mix{j + 3}"] = ("lo", LO["lora"] + j + 1)
LAST_READ["dil"] = LAST_READ["dilB"]


def rw_tiles(c):
    at, t = LO["rwkv"] + c * RW_TILES, {}

    def add(*key):
        nonlocal at
        t[key] = at
        at += 1

    add("kk")
    add("V")
    for z in (0, 1):
        add("wa", z)
    for z in (0, 1):
        for k in ("A0", "A1", "B0", "B1", "K0", "K1"):
            add(k, z)
    for lev in range(1, RW_LEVELS + 1):
        for z in (0, 1):
            add("W", lev, z)
        for z in (0, 1):
            add("X", lev, z)
            if lev < RW_LEVELS:
                add("Y", lev, z)
    for z in (0, 1):
        add("BK", z)
    for ji in (0, 1):
        for k in ("Z", "P", "R", "U"):
            for z in (0, 1):
                add(k, ji, z)
        if ji == 0:
            for z in (0, 1):
                add("S", z)
    for k in ("mean", "var", "g"):
        for z in (0, 1):
            add(k, z)
    assert at == LO["rwkv"] + (c + 1) * RW_TILES
    return t


def build(nc, d, out_d, stop=None, dump=None):
    ctx = ExitStack()
    with ctx:
        def sb(name, shape, dt=F32):
            return ctx.enter_context(nc.sbuf_tensor(name, shape, dt))

        def sem(name):
            return ctx.enter_context(nc.semaphore(name))

        ring = sb("ring", [P, RING, BLK])
        wh = sb("wh", [P, PREP, BLK], F32R)
        wl = sb("wl", [P, PREP, BLK], F32R)
        x = sb("x", [P, C, S])
        spare0 = nc.sbuf_base
        hh = sb("hh", [P, C, S], F32R)
        hl = sb("hl", [P, C, S], F32R)
        hidh = sb("hidh", [P, 2, 512], F32R)
        hidl = sb("hidl", [P, 2, 512], F32R)
        spare = nc.alloc_sbuf_tensor_at("spare", [P, 6144], F32, offset=spare0)
        cols = sb("cols", [P, NCOLS])
        mats = sb("mats", [P, MATS_A.shape[1]])
        rows = sb("rows", [1, 72])
        zero = sb("zero", [1, P])
        mod = sb("mod", [P, 2, 48])
        small = sb("small", [P, 4 * C + 4 * C + C + C])
        ARENA = 26200
        arena = sb("arena", [P, ARENA])
        ps = ctx.enter_context(nc.psum_tensor("ps", [P, 8, 512], F32))

        def col(name, j=0, n=1):
            return cols[:, COLS[name][0] + j:COLS[name][0] + j + n]

        def mat(name):
            return mats[:, MATS[name][0]:MATS[name][0] + MATS[name][1]]

        ident, ones, blk64, rotm = mat("ident"), mat("ones"), mat("blk64"), mat("rot")
        gm = small[:, 0:32].rearrange("p (i c) -> p i c", i=4)
        neg0 = small[:, 32:64]
        omka = small[:, 64:72]
        silc = small[:, 72:80]

        class Area:

            def __init__(s, t, at, end):
                s.t, s.at, s.end = t, at, end

            def fits(s, n):
                return s.at + n <= s.end

            def take(s, n):
                assert s.fits(n), (s.at, n, s.end)
                s.at += n
                return s.t[:, s.at - n:s.at]

        FREE0 = 4624
        HF = arena[:, 0:C * 258].rearrange("p (c s) -> p c s", c=C)
        hf = HF[:, :, 1:257]
        SQ = arena[:, 2064:4112].rearrange("p (c s) -> p c s", c=C)
        STD = arena[:, 4112:4368]
        RST = arena[:, 4368:4624]

        keep = Area(arena, ARENA - 13568, ARENA)
        rT, kT, vT = (keep.take(C * S).rearrange("p (c s) -> p c s", c=C) for _ in range(3))
        lora2 = keep.take(4096)
        th = keep.take(1024).rearrange("p (j s) -> p j s", j=4)
        rwm = keep.take(2304)

        def rmask(name):
            return rwm[:, RWM[name][0]:RWM[name][0] + P]

        mixa = Area(arena, FREE0, ARENA - 13568)
        xx = mixa.take(C * S).rearrange("p (c s) -> p c s", c=C)
        mixb = mixa.take(C * S).rearrange("p (c s) -> p c s", c=C)
        lex = mixa.take(512)

        wa_, wb_ = Area(arena, 0, ARENA - 13568), Area(spare, 0, 6144)

        def work(n):
            return (wa_ if wa_.fits(n) else wb_).take(n)

        RW = []
        for z in (0, 1):
            b = {}
            for name, n in (("A", 512), ("Al", 512), ("X", 512), ("Y", 512), ("W", 512), ("N6", 512), ("Arb", 512),
                            ("Ark", 512), ("Aak", 512), ("ea", 512), ("cum", 256), ("cc", 256), ("cx", 256), ("E", 768),
                            ("ar", 512), ("bt", 256), ("kt", 256), ("BK", 256), ("Z", 128), ("P0", 128), ("R", 128),
                            ("U", 128), ("S0", 128), ("fac", 2)):
                b[name] = work(n)
            RW.append(b)
        kkc, ksq, Vt, kkn = work(256), work(256), work(256), work(256)
        rkr = work(256)

        cs, rw_side, at_side, cmp_side = sem("constants_landed"), sem("rwkv_side_landed"), sem("att_side_landed"), sem("cmp_landed")
        landed = [sem(f"landed{i}") for i in range(RING)]
        ada_used, wh_ready, w_ready, down_used = sem("ada_used"), sem("wh_ready"), sem("w_ready"), sem("down_used")
        tile_ready = {"lo": sem("lo_ready"), "hi": sem("hi_ready")}
        tile_free = {g: [sem(f"{g}_free{i}") for i in range(4)] for g in ("lo", "hi")}
        bank0 = {"lo": 0, "hi": 4}
        src_ready, hh_ready, h_ready = sem("src_ready"), sem("hh_ready"), sem("h_ready")
        named = {}

        def ev(name):
            if name not in named:
                named[name] = sem(name)
            return named[name]

        done_sem = {"lo": tile_ready["lo"], "down": down_used}

        def tile(g, m):
            return ps[:, bank0[g] + m % 4, :]

        def ready(eng, g, m, plus=0):
            eng.wait_ge(tile_ready[g], m + 1 + plus)

        def free(g, m):
            return tile_free[g][m % 4]

        order = ["ada", "norm_tm0", "mix", "rwkv", "rwo", "moe0", "norm_tm1", "dilA", "att_dilA", "dilB", "att_dilB", "dilo", "moe1",
                 "norm_final", "norm_at0", "nsa", "nsapost", "att_nsa", "nsao", "mlp0", "norm_at1", "sb", "att_sb", "sbo", "mlp1",
                 "norm_at2", "conv", "convn", "convo", "mlp2", "norm_at3", "moba", "mobapost", "att_moba", "mobao", "mlp3"]
        if stop:
            order = order[:order.index(stop) + 1]
        last_q = 0
        for name in order:
            for nm, k in ORDER:
                if nm == name or (name == "mix" and nm in ("rkv", "lora")):
                    last_q = Q0[nm] + k
        NS = last_q
        NB = ADA + NS

        LOOP = {"moe": 8, "mlp": 4}

        def dump_view(name):
            return {"hf": hf, "rT": rT, "kT": kT, "vT": vT, "x": x, "mod": None}[name]

        block = ctx.enter_context(nc.Block())

        @block.sync
        def _(sp):
            def load(n, it=None):
                s = n % RING
                src = d["stream"][n:n + 1] if it is None else d["stream"][bass.ds(it * RING + s, 1)]
                sp.dma_start(ring[:, s, :], src.rearrange("a p n -> (a p) n")).then_inc(landed[s], 16)

            for n in range(RING):
                load(n)
            with sp.Fori(1, ADA // RING + 1) as it:
                for s in range(RING):
                    sp.wait_ge(ada_used, it * RING + (s - RING + 1))
                    load(s, it)
            full = NB // RING
            if full > ADA // RING + 1:
                with sp.Fori(ADA // RING + 1, full) as it:
                    for s in range(RING):
                        sp.wait_ge(w_ready, it * RING + (s - RING - ADA + 1))
                        load(s, it)
            for n in range(full * RING, NB):
                sp.wait_ge(w_ready, n - RING - ADA + 1)
                load(n)
            sp.wait_ge(ev("result_ready"), 1)
            src = x if dump is None else dump_view(dump)
            sp.dma_start(out_d, src[:, :, :]).then_inc(ev("result_stored"), 16)
            sp.wait_ge(ev("result_stored"), 16)
            sp.wait_ge(rw_side, 32)
            if "rwkv" in order:
                sp.wait_ge(at_side, 16)

        def wait_done(eng, what, it=None, per=None):
            kind, n = what
            if it is None:
                eng.wait_ge(done_sem[kind], n)
            else:
                eng.wait_ge(done_sem[kind], it * per[kind] + n)

        ata = Area(arena, FREE0, ARENA)
        atm = ata.take(ATM_A.shape[1])

        def amask(name):
            return atm[:, ATM[name][0]:ATM[name][0] + ATM[name][1]]

        def areas(at, *sizes):
            a = Area(arena, at, ARENA)
            return [a.take(n) for n in sizes] + [a.at]

        AT0 = ata.at
        Sj0, Sj1, Pt, Tb, Ub, MxDn, AT1 = areas(AT0, 768, 768, 768, 768, 768, 32, )
        Sj = (Sj0, Sj1)
        QK, VV, AT2 = areas(AT1, 6144, 3072)
        QK = QK.rearrange("p (n s) -> p n s", s=S)
        VV = VV.rearrange("p (n t e) -> p n t e", t=2, e=256)
        WC = areas(AT1 + 5120, 8192)[0].rearrange("p (j l e) -> p j l e", j=2, l=32)
        KP = arena[:, 2064:2064 + 1920].rearrange("p (j l g n) -> p j l g n", j=2, l=32, g=2)
        CMP = areas(AT1 + 5120 + 8192, 32)[0]
        VCMP = STD
        GB, T0a, T1, Lr, Gt, MO, _ = areas(AT0, EXPERTS * S, 1024, 512, 72, 64, 400)
        GB = GB.rearrange("p (e s) -> p e s", s=S)
        T0 = T0a.rearrange("p (b n) -> p b n", b=2)
        Lr = Lr.rearrange("p (t n) -> p t n", t=2)
        Gt = Gt.rearrange("p (t n) -> p t n", t=2)
        CU, CA, CT, CE, CO = areas(AT0, C * 286, C * S, C * S, 1024)
        CU = CU.rearrange("p (c s) -> p c s", c=C)
        CA = CA.rearrange("p (c s) -> p c s", c=C)
        CT = CT.rearrange("p (c s) -> p c s", c=C)

        Q_OF = {"dil": lambda g, h4: (g * 2 + 0) * 4 + h4}

        def lin_of(name):
            out = []
            for j, (q, m) in enumerate(zip(range(Q0[name], Q0[name] + dict(ORDER)[name]), range(LO[name], 10 ** 9))):
                tokens = ((name in ("dilA", "dilB") and j % 6 >= 4) or (name == "nsa" and j in (7, 9))
                          or (name in ("sb", "moba") and j >= 8))
                out.append((j, q, m, "t" if tokens else "f"))
            return out

        def dil_job(j):
            return j // 2, j % 2

        VN = areas(AT1 + 4096, 1024)[0].rearrange("p (n t e) -> p n t e", t=2, e=256)
        GATES = RST[:, 0:48].rearrange("p (t n) -> p t n", t=2)
        Rb = Sj0
        Ab_ = Pt[:, 256:512]
        SCALE = float(DH) ** -0.5
        POST0 = {"nsapost": 0, "mobapost": 7}
        HID0 = {"moe0": 0, "moe1": 32, "mlp0": 64, "mlp1": 80, "mlp2": 96, "mlp3": 112}
        CS_N = 64
        PAIRS = {"nsapost": [(0, ("nsa_q", 0)), (2, ("nsa_q", 0)), (4, ("nsa_q", 0)), (6, ("nsa_q", 0)), (8, ("nsa_k", 0)),
                             (12, ("nsa_k", 1)), (14, ("nsa_k", 2))],
                 "mobapost": [(i, ("moba_q" if i < 8 else "moba_k", 0)) for i in range(0, 16, 2)]}

        def seg(a, qt):
            return slice(qt * P, (qt + 1) * P)

        def plain(h, qt, m):
            return [(m, [(0, S, QK[:, h, qt * P:(qt + 1) * P], QK[:, 8 + h, :])])]

        def plain_flips(h, qt, m, s):
            return [(m, [(P, 0, s[:, 0:P]), (P, P, s[:, P:2 * P])])]

        def plain_values(h):
            return [(VV[:, h // 2, t, (h % 2) * P:(h % 2 + 1) * P], Pt[:, t * P:(t + 1) * P]) for t in range(2)]

        def dil_scores(h, qt, m):
            p = [QK[:, 8 * g + h, qt * P:(qt + 1) * P] for g in range(3)]
            return [(m, [(0, S, p[0], QK[:, 4 + h, :]), (S, S, p[1], QK[:, 12 + h, :])]), (m + 1, [(0, S, p[2], QK[:, 20 + h, :])])]

        def dil_flips(h, qt, m, s):
            return [(m, [(P, i * P, s[:, i * P:(i + 1) * P]) for i in range(4)]),
                    (m + 1, [(P, i * P, s[:, (4 + i) * P:(5 + i) * P]) for i in range(2)])]

        def dil_values(h):
            return [(VV[:, 2 * g + h // 2, t, (h % 2) * P:(h % 2 + 1) * P], Pt[:, (2 * g + t) * P:(2 * g + t + 1) * P])
                    for g in range(3) for t in range(2)]

        def nsa_scores(h, qt, m):
            q_, g = QK[:, h, qt * P:(qt + 1) * P], h // 4
            return [(m, [(0, S, q_, QK[:, 12 + g, :]), (S, S, q_, QK[:, 14 + g, :])]),
                    (m + 1, [(0, N_CMP, q_, CMP[:, 16 * g:16 * g + N_CMP])])]

        def nsa_flips(h, qt, m, s):
            return [(m, [(P, i * P, s[:, i * P:(i + 1) * P]) for i in range(4)]), (m + 1, [(N_CMP, 0, s[:, 512:512 + N_CMP])])]

        def nsa_values(h):
            g = h // 4
            v = [(VN[:, b, t, g * P:(g + 1) * P], Pt[:, (2 * b + t) * P:(2 * b + t + 1) * P]) for b in range(2) for t in range(2)]
            return v + [(VCMP[0:N_CMP, g * P:(g + 1) * P], Pt[0:N_CMP, 512:512 + P])]

        def score_tile(name, j):
            k = ATT[name]["lo"] // 2
            return LO["att_" + name] + (0 if j == 0 else k + (j - 1) * 2 * k)

        def flip_tile(name, j):
            k = ATT[name]["lo"] // 2
            return LO["att_" + name] + k + j * 2 * k + (k if j + 1 < ATT[name]["jobs"] else 0)

        ATT = {
            "dilA": dict(base="dil", first=0, jobs=8, lo=4, scores=dil_scores, flips=dil_flips, values=dil_values, head0=0,
                         soft=[(0, 768)], n=1),
            "dilB": dict(base="dil", first=8, jobs=8, lo=4, scores=dil_scores, flips=dil_flips, values=dil_values, head0=4,
                         soft=[(0, 768)], n=2),
            "nsa": dict(base="nsa", first=16, jobs=16, lo=4, scores=nsa_scores, flips=nsa_flips, values=nsa_values, head0=0,
                        soft=[(0, S), (S, 2 * S), (512, 512 + N_CMP)], n=3),
            "sb": dict(base="sb", first=32, jobs=16, lo=2, scores=plain, flips=plain_flips, values=plain_values, head0=0,
                       soft=None, n=4),
            "moba": dict(base="moba", first=48, jobs=16, lo=2, scores=plain, flips=plain_flips, values=plain_values, head0=0,
                         soft=[(0, S)], n=5),
        }
        for _a in ATT.values():
            _a["pe_waits"] = lambda eng, _a=_a: eng.wait_ge(ev("qkv_done"), _a["n"])

        @block.tensor
        def _(pe):
            mm = nc.tensor.matmul
            skips = {}

            def claim(g, m, it=None, per=0):
                if it is not None:
                    pe.wait_ge(free(g, m), it * (per // 4) + m // 4)
                elif m >= 4:
                    pe.wait_ge(free(g, m), m // 4)
                return tile(g, m)

            def skip(name):
                for m in range(LO[name] - SKIP[name], LO[name]):
                    pe.wait_ge(tile_ready["lo"], m)
                    claim("lo", m)
                    pe.sem_inc(tile_ready["lo"], 1)
                    pe.sem_inc(free("lo", m), 1)

            def three(out, w, h, first, last):
                mm(out, w[0], h[0], start=first, stop=False)
                mm(out, w[1], h[0], start=False, stop=False)
                return mm(out, w[0], h[1], start=False, stop=last)

            def linear(q, m, kind="f", half=None, tile_=None):
                pe.wait_ge(w_ready, q + 1)
                t = claim("lo", m)
                s = q % PREP
                W = [w[:, s, :].rearrange("p (k n) -> p k n", k=C) for w in (wh, wl)]
                for j in ((0, 1) if half is None else (half,)):
                    o = t[:, 0:S] if half is not None else t[:, j * S:(j + 1) * S]
                    for k in range(C):
                        if kind == "f":
                            last = three(o, [w[:, k, j * P:(j + 1) * P] for w in W], [h[:, k, :] for h in (hh, hl)], k == 0, k == C - 1)
                        else:
                            a = [h[:, k, j * P:(j + 1) * P] for h in (hh, hl)]
                            mm(o, a[0], W[0][:, k, :], start=k == 0, stop=False)
                            mm(o, a[1], W[0][:, k, :], start=False, stop=False)
                            last = mm(o, a[0], W[1][:, k, :], start=False, stop=k == C - 1)
                last.then_inc(tile_ready["lo"], 1)

            def wait_h(name):
                pe.wait_ge(h_ready, 4 * (VER[name] + 1))

            def linears(name, version=None):
                wait_h(version or name)
                for _, q, m, kind in lin_of(name):
                    linear(q, m, kind)

            def norm(name):
                k = NORMS.index(name)
                pe.wait_ge(ev("squares"), k + 1)
                t = claim("lo", LO["norm_" + name])
                for c in range(C):
                    last = mm(t[:, 0:S], ones, SQ[:, c, :], start=c == 0, stop=c == C - 1)
                last.then_inc(tile_ready["lo"], 1)

            def ada_all():
                pe.wait_ge(ev("silu_c"), 1)
                t = claim("lo", LO["ada"])
                for n in range(ADA):
                    s = n % RING
                    pe.wait_ge(landed[s], 16 * (n // RING + 1))
                    W = ring[:, s, :].rearrange("p (k n) -> p k n", k=C)
                    for j in range(2):
                        for k in range(C):
                            last = mm(t[:, 2 * n + j:2 * n + j + 1], W[:, k, j * P:(j + 1) * P], silc[:, k:k + 1],
                                      start=k == 0, stop=k == C - 1)
                    last.then_inc(ada_used, 1)
                pe.wait_ge(ada_used, ADA)
                pe.sem_inc(tile_ready["lo"], 1)

            def mix():
                for j in range(3):
                    wait_h(f"mix{j}")
                    for i in range(4):
                        linear(Q0["rkv"] + 4 * j + i, LO["rkv"] + 4 * j + i)
                wait_h("mix3")
                linear(Q0["lora"], LO["lora"], half=0)
                wait_h("mix4")
                linear(Q0["lora"], LO["lora"] + 1, half=1)
                wait_h("mix5")
                linear(Q0["lora"] + 1, LO["lora"] + 2)

            def rwkv():
                pe.wait_ge(ev("lora_ready"), 3)
                pe.wait_ge(ev("rkv_ready"), 12)
                for c in range(C):
                    T = rw_tiles(c)

                    def cl(*key):
                        return claim("lo", T[key])

                    def fin(ins, g="lo"):
                        ins.then_inc(tile_ready[g], 1)

                    n = 2 * c
                    pe.wait_ge(ev("rw_ksq"), c + 1)
                    fin(mm(cl("kk")[:, 0:S], blk64, ksq, start=True, stop=True))
                    t = cl("V")
                    for j in range(2):
                        last = nc.tensor.transpose(t[:, j * P:(j + 1) * P], vT[:, c, j * P:(j + 1) * P], ident)
                    fin(last)
                    for z in (0, 1):
                        t = cl("wa", z)
                        for i in range(2):
                            lo_ = 64 * z
                            last = mm(t[:, i * S:(i + 1) * S], lora2[lo_:lo_ + 64, i * D + c * P:i * D + (c + 1) * P],
                                      th[lo_:lo_ + 64, i, :], start=True, stop=True)
                        fin(last)
                    for z in (0, 1):
                        b = RW[z]
                        pe.wait_ge(ev("rw_feat"), n + z + 1)
                        ar = b["ar"].rearrange("p (i s) -> p i s", i=2)
                        th_ = claim("hi", HI["rwkv"] + 4 * c + z)
                        fin(mm(th_[:, 0:S], blk64, b["cx"], start=True, stop=True), "hi")
                        for h in (0, 1):
                            t = cl(f"A{h}", z)
                            for j in (0, 1):
                                r = slice(64 * h, 64 * h + 64)
                                last = mm(t[:, j * P:(j + 1) * P], ar[r, 0, j * P:(j + 1) * P],
                                          b["bt"][r, j * P:(j + 1) * P], start=True, stop=True)
                            fin(last)
                        for k, src in (("B", "bt"), ("K", "kt")):
                            for h in (0, 1):
                                t = cl(f"{k}{h}", z)
                                r = slice(64 * h, 64 * h + 64)
                                for j in (0, 1):
                                    last = mm(t[:, 2 * j * P:2 * (j + 1) * P], b[src][r, j * P:(j + 1) * P],
                                              ar[r, :, j * P:(j + 1) * P], start=True, stop=True)
                                fin(last)
                    for lev in range(1, RW_LEVELS + 1):
                        for z in (0, 1):
                            b = RW[z]
                            pe.wait_ge(ev("rw_al"), 12 * c + (2 + 2 * z if lev == 1 else 4 + 2 * (lev - 2) + z + 1))
                            if lev == 1:
                                pe.wait_ge(ev("rw_x"), n + z + 1)
                            else:
                                pe.wait_ge(ev("rw_xy"), (c * RW_LEVELS + lev - 2) * 2 + z + 1)
                            t = cl("W", lev, z)
                            for p in range(4):
                                q_ = slice(p * P, (p + 1) * P)
                                last = mm(t[:, q_], b["Al"][:, q_], b["X"][:, q_], start=True, stop=True)
                            fin(last)
                        for z in (0, 1):
                            b = RW[z]
                            pe.wait_ge(ev("rw_w1"), (c * RW_LEVELS + lev - 1) * 2 + z + 1)
                            t = cl("X", lev, z)
                            for p in range(4):
                                q_ = slice(p * P, (p + 1) * P)
                                last = mm(t[:, q_], b["Y"][:, q_], b["W"][:, q_], start=True, stop=True)
                            fin(last)
                            if lev < RW_LEVELS:
                                t = cl("Y", lev, z)
                                for p in range(4):
                                    q_ = slice(p * P, (p + 1) * P)
                                    last = mm(t[:, q_], b["W"][:, q_], b["Y"][:, q_], start=True, stop=True)
                                fin(last)
                    for z in (0, 1):
                        b = RW[z]
                        j = z
                        t = cl("BK", z)
                        nc.tensor.transpose(t[:, 0:P], b["bt"][:, j * P:(j + 1) * P], ident)
                        fin(nc.tensor.transpose(t[:, P:2 * P], b["kt"][:, j * P:(j + 1) * P], ident))
                    pe.wait_ge(ev("rw_v"), c + 1)
                    for ji in (0, 1):
                        n4 = (c * 2 + ji) * 2
                        V = Vt.rearrange("p (j n) -> p j n", j=2)

                        def m4(name, z, h, j):
                            return RW[z][name][:, (2 * h + j) * P:(2 * h + j + 1) * P]

                        for z in (0, 1):
                            b, j = RW[z], (z if ji == 0 else 1 - z)
                            ar = b["ar"].rearrange("p (i s) -> p i s", i=2)
                            if ji == 0:
                                pe.wait_ge(ev("rw_xy"), (c * RW_LEVELS + RW_LEVELS - 1) * 2 + z + 1)
                            else:
                                pe.wait_ge(ev("rw_s"), n + z + 1)
                            t = cl("Z", ji, z)
                            if ji:
                                mm(t[:, 0:P], ar[:, 0, j * P:(j + 1) * P], b["S0"], start=True, stop=False, skip_group_check=True)
                            for h in (0, 1):
                                last = mm(t[:, 64 * h:64 * h + 64], m4("Aak", z, h, j), V[:, j, 64 * h:64 * h + 64],
                                          start=ji == 0, stop=True, skip_group_check=True)
                            fin(last)
                        for k, evn, lhs, rhs in (("P", "rw_z", "X", "Z"), ("R", "rw_p", "N6", "P0"), ("U", "rw_r", "X", "R")):
                            for z in (0, 1):
                                b, j = RW[z], (z if ji == 0 else 1 - z)
                                pe.wait_ge(ev(evn), n4 + z + 1)
                                t = cl(k, ji, z)
                                for h in (0, 1):
                                    last = mm(t[:, 64 * h:64 * h + 64], m4(lhs, z, h, j), b[rhs][:, 64 * h:64 * h + 64],
                                              start=True, stop=True)
                                fin(last)
                        for z in (0, 1):
                            b, j = RW[z], (z if ji == 0 else 1 - z)
                            ar = b["ar"].rearrange("p (i s) -> p i s", i=2)
                            pe.wait_ge(ev("rw_u"), n4 + z + 1)
                            m = HI["rwkv"] + 4 * c + 2 + z
                            t = claim("hi", m) if ji == 0 else tile("hi", m)
                            if ji:
                                mm(t[:, j * P:(j + 1) * P], b["S0"], ar[:, 1, j * P:(j + 1) * P], start=True, stop=False,
                                   skip_group_check=True)
                            for h in (0, 1):
                                r = slice(64 * h, 64 * h + 64)
                                o = t[r, j * P:(j + 1) * P]
                                mm(o, b["U"][:, r], m4("Arb", z, h, j), start=ji == 0, stop=False, skip_group_check=True)
                                last = mm(o, V[:, j, r], m4("Ark", z, h, j), start=False, stop=True, skip_group_check=True)
                            if ji:
                                fin(last, "hi")
                        if ji == 0:
                            for z in (0, 1):
                                b, j = RW[z], z
                                pe.wait_ge(ev("rw_bk"), n + z + 1)
                                t = cl("S", z)
                                for h in (0, 1):
                                    r = slice(64 * h, 64 * h + 64)
                                    BK = b["BK"]
                                    mm(t[r, 0:64], BK[:, 64 * h:64 * h + 64], b["U"][:, r], start=True, stop=False)
                                    last = mm(t[r, 0:64], BK[:, P + 64 * h:P + 64 * h + 64], V[:, j, r], start=False, stop=True)
                                fin(last)
                    for k, evn, src in (("mean", "rw_ys", "cum"), ("var", "rw_dsq", "E")):
                        for z in (0, 1):
                            pe.wait_ge(ev(evn), n + z + 1)
                            fin(mm(cl(k, z)[:, 0:S], blk64, RW[z][src][:, 0:S], start=True, stop=True))
                    for z in (0, 1):
                        fin(mm(cl("g", z)[:, 0:S], lora2[:, (2 + z) * D + c * P:(2 + z) * D + (c + 1) * P], th[:, 2 + z, :],
                               start=True, stop=True))

            def accumulate(name):
                moe = name[:3] == "moe"
                ups, n, per = (2, EXPERTS, 8) if moe else (1, UNITS, 4)
                q0, m0, d0 = Q0[name], LO[name], DOWN0[name]
                loop = {"lo": per, "down": 4, "q": 4 * (ups + 1)}
                skip(name)
                wait_h(name)
                for i in range(4):
                    t = claim("hi", HI[name] + i)
                    mm(t, zero[0:1, :], zero[0:1, 0:1].to_broadcast([1, 512]), start=True, stop=False, skip_group_check=True)

                def up(q, m, it):
                    for u in range(ups):
                        if it is None:
                            pe.wait_ge(w_ready, q + u + 1)
                        else:
                            pe.wait_ge(w_ready, it * loop["q"] + (q + u + 1))
                        t = claim("lo", m + u, it, per)
                        W = [w[:, (q + u) % PREP, :].rearrange("p (k n) -> p k n", k=C) for w in (wh, wl)]
                        for j in range(2):
                            for k in range(C):
                                last = three(t[:, j * S:(j + 1) * S], [w[:, k, j * P:(j + 1) * P] for w in W],
                                             [h[:, k, :] for h in (hh, hl)], k == 0, k == C - 1)
                        last.then_inc(tile_ready["lo"], 1)

                def down(e, q, it):
                    hid = HID0[name] + e + 1
                    if it is None:
                        pe.wait_ge(w_ready, q + 1)
                        pe.wait_ge(ev("hidden"), hid)
                    else:
                        pe.wait_ge(w_ready, it * loop["q"] + (q + 1))
                        pe.wait_ge(ev("hidden"), it * 4 + hid)
                    W = [w[:, q % PREP, :].rearrange("p (f n) -> p f n", f=2) for w in (wh, wl)]
                    H = [h[:, e % 2, :].rearrange("p (f s) -> p f s", f=2) for h in (hidh, hidl)]
                    for c in range(C):
                        o = tile("hi", HI[name] + c // 2)[:, (c % 2) * S:(c % 2 + 1) * S]
                        for f in range(2):
                            for a, b in ((0, 0), (1, 0), (0, 1)):
                                last = mm(o, W[a][:, f, c * P:(c + 1) * P], H[b][:, f, :], start=False, stop=False,
                                          skip_group_check=True)
                    last.then_inc(down_used, 1)

                def step(e, it=None):
                    b = q0 + ups + e * (ups + 1)
                    if e + 1 < n:
                        up(b, m0 + ups * (e + 1), it)
                        down(e, b + ups, it)
                    else:
                        down(e, b, it)

                up(q0, m0, None)
                with pe.Fori(0, n // 4 - 1) as it:
                    for e in range(4):
                        step(e, it)
                for e in range(n - 4, n):
                    step(e)
                pe.wait_ge(down_used, d0 + n)
                pe.sem_inc(tile_ready["hi"], 4)

            def route(i):
                t = claim("lo", LO[f"route{i}"])
                pe.wait_ge(src_ready, 4 * (VER[f"moe{i}"] + 1))
                for tt in range(2):
                    o = t[:, tt * 36:tt * 36 + 36]
                    for k in range(C):
                        mm(o, hf[:, k, tt * P:(tt + 1) * P], col(f"router{i}", 36 * k, 36), start=k == 0, stop=False)
                    last = mm(o, ones[0:1, :], rows[0:1, 36 * i:36 * i + 36], start=False, stop=True)
                last.then_inc(tile_ready["lo"], 1)
                pe.wait_ge(ev("gates"), i + 1)
                for pr in range(EXPERTS // 2):
                    t = claim("lo", LO[f"gate{i}"] + pr)
                    for e in range(2):
                        for tt in range(2):
                            g = Gt[:, tt, 2 * pr + e:2 * pr + e + 1].to_broadcast([P, P])
                            last = mm(t[:, e * S + tt * P:e * S + (tt + 1) * P], g, ident, start=True, stop=True)
                    last.then_inc(tile_ready["lo"], 1)

            def attention(name):
                J = ATT[name]
                base, b0 = J["base"], J["first"]

                def scores(j):
                    h, qt = j // 2, j % 2
                    for m, parts in J["scores"](h, qt, score_tile(name, j)):
                        t = claim("lo", m)
                        for at, n, q_, k_ in parts:
                            last = mm(t[:, at:at + n], q_, k_, start=True, stop=True)
                        last.then_inc(tile_ready["lo"], 1)

                def flip(j):
                    h, qt = j // 2, j % 2
                    pe.wait_ge(ev("probs"), b0 + j + 1)
                    for m, parts in J["flips"](h, qt, flip_tile(name, j), Sj[(b0 + j) % 2]):
                        t = claim("lo", m)
                        for rows_, at, src in parts:
                            last = nc.tensor.transpose(t[0:rows_, at:at + P], src, ident)
                        last.then_inc(tile_ready["lo"], 1)

                def outs(j):
                    h, qt = j // 2, j % 2
                    pe.wait_ge(ev("flipped"), b0 + j + 1)
                    m = HI["att_" + name] + j // 2
                    t = claim("hi", m) if qt == 0 else tile("hi", m)
                    vs = J["values"](h)
                    for i, (v, p_) in enumerate(vs):
                        last = mm(t[:, qt * P:(qt + 1) * P], v, p_, start=i == 0, stop=i == len(vs) - 1)
                    last.then_inc(tile_ready["hi"] if qt else ev("half_out"), 1)

                n = J["jobs"]
                J["pe_waits"](pe)
                scores(0)
                for j in range(n):
                    if j + 1 < n:
                        scores(j + 1)
                    flip(j)
                    outs(j)

            def post(name, n):
                for i in range(n):
                    k = POST0[name] + i
                    pe.wait_ge(ev("qk_sq"), k + 1)
                    t = claim("lo", LO[name] + 2 * i)
                    mm(t, ones, Tb[:, 0:512], start=True, stop=True).then_inc(tile_ready["lo"], 1)
                    pe.wait_ge(ev("qk_norm"), k + 1)
                    t = claim("lo", LO[name] + 2 * i + 1)
                    mm(t, rotm, Ub[:, 0:512], start=True, stop=True).then_inc(tile_ready["lo"], 1)

            def nsa_gate():
                t = claim("lo", LO["nsagate"])
                for tt in range(2):
                    for k in range(C):
                        last = mm(t[:, tt * 24:tt * 24 + 24], hf[:, k, tt * P:(tt + 1) * P], col("nsa_gate", 24 * k, 24),
                                  start=k == 0, stop=k == C - 1)
                last.then_inc(tile_ready["lo"], 1)

            def nsa_compress():
                pe.wait_ge(cmp_side, 16)
                pe.wait_ge(ev("kp"), 1)
                t = claim("lo", LO["nsacmp"])
                o = t[:, 0:2 * N_CMP].rearrange("p (g n) -> p g n", g=2)
                for l in range(32):
                    last = mm(o, WC[:, 0, l, :], KP[:, 0, l, :, :], start=l == 0, stop=l == 31)
                last.then_inc(tile_ready["lo"], 1)
                t = claim("hi", HI["nsacmp"])
                for g in range(2):
                    for l in range(32):
                        last = mm(t[0:N_CMP, g * P:(g + 1) * P], KP[:, 1, l, g, :], WC[:, 1, l, :], start=l == 0, stop=l == 31)
                last.then_inc(tile_ready["hi"], 1)

            def conv_norm():
                for i, evn in enumerate(("conv_out", "conv_sq")):
                    pe.wait_ge(ev(evn), 1)
                    t = claim("lo", LO["convn"] + i)
                    for c in range(C):
                        last = mm(t[:, 0:S], ones, (CA if i == 0 else SQ)[:, c, :], start=c == 0, stop=c == C - 1)
                    last.then_inc(tile_ready["lo"], 1)

            pe.wait_ge(cs, CS_N)
            steps = {"ada": ada_all, "mix": mix, "rwkv": rwkv, "nsapost": lambda: (nsa_gate(), post("nsapost", 7), nsa_compress()),
                     "mobapost": lambda: post("mobapost", 8), "convn": conv_norm,
                     "moe0": lambda: (norm("cm0"), route(0), accumulate("moe0")),
                     "moe1": lambda: (norm("cm1"), route(1), accumulate("moe1"))}
            for i in range(4):
                steps[f"mlp{i}"] = lambda i=i: (norm(f"ml{i}"), accumulate(f"mlp{i}"))
            for name in order:
                if name in steps:
                    steps[name]()
                elif name.startswith("norm_"):
                    norm(name[5:])
                elif name.startswith("att_"):
                    attention(name[4:])
                else:
                    linears(name, "dil" if name in ("dilA", "dilB") else None)

        @block.scalar
        def _(act):
            chain, own = sem("act_chain"), [0]

            def K(ins, it=None, per=0):
                own[0] += 1
                ins.then_inc(chain, 1)
                act.wait_ge(chain, own[0] if it is None else it * per + own[0])

            def fn(out, in_, f, scale=1.0, bias=0.0, **k):
                return nc.scalar.activation(out, in_, f, scale=scale, bias=bias, **k)

            def copy(out, in_):
                return nc.scalar.activation(out, in_, ACT.Copy)

            def prep(q, it=None, loop=None):
                if q >= NS:
                    return
                n = ADA + q
                s = n % RING
                at = 16 * (n // RING + 1)
                act.wait_ge(landed[s], at if it is None else it * (16 * loop["q"] // RING) + at)
                if q >= PREP:
                    wait_done(act, DONE[q - PREP], it, loop)
                copy(wh[:, q % PREP, :], ring[:, s, :]).then_inc(wh_ready, 1)

            def split(name, src):
                v = VER[name]
                if v:
                    wait_done(act, LAST_READ[VERSIONS[v - 1]])
                for i in range(4):
                    act.wait_ge(src_ready, 4 * v + i + 1)
                    copy(hh[:, 2 * i:2 * i + 2, :], src[:, 2 * i:2 * i + 2, :]).then_inc(hh_ready, 1)

            def norm(name):
                k, m = NORMS.index(name), LO["norm_" + name]
                if k:
                    act.wait_ge(ev("x_ready"), k)
                fn(SQ, x[:, :, :], ACT.Square).then_inc(ev("squares"), 1)
                ready(act, "lo", m)
                K(fn(STD, tile("lo", m)[:, 0:S], ACT.Ln, scale=1.0 / D, bias=EPS))
                act.sem_inc(free("lo", m), 1)
                fn(RST, STD, ACT.Exp, scale=-0.5).then_inc(ev("rstd"), 1)

            def only_prep(name):
                for j in range(dict(ORDER)[name]):
                    prep(Q0[name] + j + PREP)

            def mix():
                act.wait_ge(rw_side, 32)
                for j in range(3):
                    split(f"mix{j}", mixb)
                    for i in range(4):
                        q, m = Q0["rkv"] + 4 * j + i, LO["rkv"] + 4 * j + i
                        ready(act, "lo", m)
                        dst = (rT, kT, vT)[j][:, 2 * i:2 * i + 2, :].rearrange("p c s -> p (c s)")
                        K(copy(dst, tile("lo", m)))
                        act.sem_inc(free("lo", m), 1)
                        act.sem_inc(ev("rkv_ready"), 1)
                        prep(q + PREP)
                m = LO["lora"]
                split("mix3", mixb)
                ready(act, "lo", m)
                K(fn(lex[:, 0:S], tile("lo", m)[:, 0:S], ACT.Exp, scale=2.0))
                act.sem_inc(free("lo", m), 1)
                act.sem_inc(ev("lora_exp"), 1)
                split("mix4", mixb)
                ready(act, "lo", m + 1)
                K(copy(th[:, 1, :], tile("lo", m + 1)[:, 0:S]))
                act.sem_inc(free("lo", m + 1), 1)
                act.sem_inc(ev("lora_ready"), 1)
                prep(Q0["lora"] + PREP)
                split("mix5", mixb)
                act.wait_ge(ev("lora_w"), 1)
                ready(act, "lo", m + 2)
                K(fn(lex, tile("lo", m + 2), ACT.Exp, scale=-1.0))
                act.sem_inc(free("lo", m + 2), 1)
                act.sem_inc(ev("lora_exp"), 1)
                prep(Q0["lora"] + 1 + PREP)

            def rwkv():
                for c in range(C):
                    T, n = rw_tiles(c), 2 * c

                    def got(key, g="lo"):
                        ready(act, g, T[key])
                        return tile(g, T[key])

                    def freed(ins, m, name, g="lo"):
                        K(ins)
                        act.sem_inc(free(g, m), 1)
                        act.sem_inc(ev(name), 1)

                    act.wait_ge(ev("rw_kkc"), c + 1)
                    fn(ksq, kkc, ACT.Square).then_inc(ev("rw_ksq"), 1)
                    freed(copy(Vt, got(("V",))[:, 0:S]), T[("V",)], "rw_v")
                    for z in (0, 1):
                        b, t = RW[z], got(("wa", z))
                        fn(b["ea"][:, 0:S], t[:, 0:S], ACT.Exp, scale=-1.0, bias=neg0[:, 8 * z + c:8 * z + c + 1])
                        freed(fn(b["ea"][:, S:2 * S], t[:, S:2 * S], ACT.Exp, scale=-1.0, bias=neg0[:, 16 + 8 * z + c:17 + 8 * z + c]),
                              T[("wa", z)], "rw_ea")
                    act.wait_ge(ev("rw_kkm"), c + 1)
                    K(fn(kkn, kkn, ACT.Ln))
                    fn(kkn, kkn, ACT.Exp, scale=-0.5).then_inc(ev("rw_kkn"), 1)
                    for z in (0, 1):
                        b = RW[z]
                        act.wait_ge(ev("rw_cc"), n + z + 1)
                        fn(b["E"][:, 0:S], b["cx"], ACT.Exp)
                        fn(b["E"][:, S:2 * S], b["cc"], ACT.Exp)
                        fn(b["E"][:, 2 * S:3 * S], b["cc"], ACT.Exp, scale=-1.0)
                        fn(b["fac"][:, 1:2], b["fac"][:, 0:1], ACT.Exp).then_inc(ev("rw_E"), 1)
                    for z in (0, 1):
                        copy(RW[z]["A"][:, 0:S], got(("A0", z))[:, 0:S]).then_inc(free("lo", T[("A0", z)]), 1)
                        freed(copy(RW[z]["A"][:, S:2 * S], got(("A1", z))[:, 0:S]), T[("A1", z)], "rw_A")
                    for lev in range(1, RW_LEVELS + 1):
                        for z in (0, 1):
                            freed(copy(RW[z]["W"], got(("W", lev, z))), T[("W", lev, z)], "rw_w1")
                    for z in (0, 1):
                        freed(copy(RW[z]["BK"], got(("BK", z))[:, 0:S]), T[("BK", z)], "rw_bk")
                    for ji in (0, 1):
                        for k, dst, name in (("Z", "Z", "rw_z"), ("P", "P0", "rw_p"), ("U", "U", "rw_u")):
                            for z in (0, 1):
                                freed(copy(RW[z][dst], got((k, ji, z))[:, 0:P]), T[(k, ji, z)], name)
                    for z in (0, 1):
                        m = HI["rwkv"] + 4 * c + 2 + z
                        ready(act, "hi", m)
                        freed(copy(RW[z]["cum"], tile("hi", m)[:, 0:S]), m, "rw_ys", "hi")
                    for z in (0, 1):
                        act.wait_ge(ev("rw_d"), n + z + 1)
                        fn(RW[z]["E"][:, 0:S], RW[z]["cc"], ACT.Square).then_inc(ev("rw_dsq"), 1)
                    for z in (0, 1):
                        E_ = RW[z]["E"][:, S:2 * S]
                        K(fn(E_, got(("var", z))[:, 0:S], ACT.Ln, scale=1.0 / 64, bias=GN_EPS))
                        act.sem_inc(free("lo", T[("var", z)]), 1)
                        fn(E_, E_, ACT.Exp, scale=-0.5).then_inc(ev("rw_rs"), 1)
                split("rwo", rT)
                act.wait_ge(ev("rwkv_done"), 1)
                act.dma_start(atm, d["atm"]).then_inc(at_side, 16)

            def route(i):
                m = LO[f"route{i}"]
                act.wait_ge(ev("group_arg"), i + 1)
                fn(MO[:, 0:8], MO[:, 0:8], ACT.Exp).then_inc(ev("group_exp"), 1)
                act.wait_ge(ev("pair_arg"), i + 1)
                fn(MO[:, 8:10], MO[:, 8:10], ACT.Exp).then_inc(ev("pair_exp"), 1)
                for pr in range(EXPERTS // 2):
                    m = LO[f"gate{i}"] + pr
                    ready(act, "lo", m)
                    copy(GB[:, 2 * pr:2 * pr + 2, :].rearrange("p e s -> p (e s)"), tile("lo", m)).then_inc(free("lo", m), 1)
                K(copy(MO[:, 398:399], MO[:, 0:1]))
                act.sem_inc(ev("gates_wide"), 1)

            def accumulate(name):
                moe = name[:3] == "moe"
                ups, n, per = (2, EXPERTS, 8) if moe else (1, UNITS, 4)
                q0, m0, d0 = Q0[name], LO[name], DOWN0[name]
                loop = {"lo": per, "down": 4, "q": 4 * (ups + 1)}
                kper = 4 * (1 if moe else 2)

                def w(sem_, v, it, per_):
                    act.wait_ge(sem_, v if it is None else it * per_ + v)

                def hidden(e, m, it):
                    hid = HID0[name] + e
                    u = e % 2
                    if it is not None or hid >= 2:
                        w(ev("hidden"), hid - 1, it, 4)
                    w(tile_ready["lo"], m + 1, it, per)
                    if moe:
                        K(fn(T0[:, u, :], tile("lo", m), ACT.Exp, scale=-1.0), it, kper)
                        act.sem_inc(ev("hid_exp"), 1)
                    else:
                        K(fn(T0[:, u, :], tile("lo", m), ACT.Relu), it, kper)
                        act.sem_inc(free("lo", m), 1)
                        K(fn(T0[:, u, :], T0[:, u, :], ACT.Square), it, kper)
                        act.sem_inc(ev("hid_wide"), 1)
                    w(ev("hid_wide"), hid + 1, it, 4)
                    if it is not None or e >= 2:
                        w(down_used, d0 + e - 1, it, 4)
                    copy(hidh[:, u, :], T1 if moe else T0[:, u, :]).then_inc(ev("hidh_ready"), 1)

                def step(e, it=None):
                    b = q0 + ups + e * (ups + 1)
                    if e + 1 < n:
                        for u in range(ups):
                            prep(b + u + PREP, it, loop)
                        hidden(e + 1, m0 + ups * (e + 1), it)
                        prep(b + ups + PREP, it, loop)
                    else:
                        prep(b + PREP, it, loop)

                for u in range(ups):
                    prep(q0 + u + PREP)
                hidden(0, m0, None)
                first = own[0]
                with act.Fori(0, n // 4 - 1) as it:
                    for e in range(4):
                        step(e, it)
                assert own[0] - first == kper
                own[0] = first + kper * (n // 4 - 1)
                for e in range(n - 4, n):
                    step(e)

            def linears(name):
                for j, q, m, kind in lin_of(name):
                    ready(act, "lo", m)
                    if name in ("dilA", "dilB"):
                        g, part, pr = j // 6, j % 6 // 2, j % 2
                        dst = VV[:, 2 * g + pr] if part == 2 else QK[:, 8 * g + 4 * part + 2 * pr:8 * g + 4 * part + 2 * pr + 2]
                    elif name == "nsa":
                        dst = VN[:, 0] if j == 7 else VN[:, 1] if j == 9 else QK[:, {8: 14}.get(j, 2 * j):{8: 14}.get(j, 2 * j) + 2]
                    else:
                        dst = VV[:, j - 8] if j >= 8 else QK[:, 2 * j:2 * j + 2]
                    copy(dst, tile("lo", m).rearrange("p (a b) -> p a b", a=2)).then_inc(free("lo", m), 1)
                    prep(q + PREP)
                if name in ("dilA", "dilB", "sb"):
                    K(copy(MxDn[:, 31:32], col("c")))
                    act.sem_inc(ev("qkv_done"), 1)

            def attention(name):
                J = ATT[name]
                b0, n = J["first"], J["jobs"]

                def m_(j):
                    return score_tile(name, j)

                def exps(j):
                    s = Sj[(b0 + j) % 2]
                    if name == "sb":
                        i = b0 + j - 32
                        if i:
                            act.wait_ge(ev("sb_arg"), i)
                        ready(act, "lo", m_(j))
                        K(fn(Tb[:, 0:S], tile("lo", m_(j))[:, 0:S], ACT.Abs, scale=SCALE))
                        K(fn(Tb[:, 0:S], Tb[:, 0:S], ACT.Exp, scale=-1.0))
                        fn(Ub[:, 0:S], Tb[:, 0:S], ACT.Ln, bias=1.0).then_inc(ev("sb_log"), 1)
                        act.wait_ge(ev("sb_arg"), i + 1)
                        fn(s[:, 0:S], s[:, 0:S], ACT.Exp).then_inc(ev("probs"), 1)
                        return
                    act.wait_ge(ev("masked"), MASK0[name] + j + 1)
                    o = 16 * ((b0 + j) % 2)
                    for i, (a, b) in enumerate(J["soft"]):
                        last = fn(s[:, a:b], s[:, a:b], ACT.Exp, bias=MxDn[:, o + i:o + i + 1], accum_out=MxDn[:, o + 4 + i:o + 5 + i])
                    last.then_inc(ev("exped"), 1)

                def flips(j):
                    k = b0 + j
                    if j:
                        if j % 2:
                            act.wait_ge(ev("half_out"), HALF0[name] + j // 2 + 1)
                        else:
                            ready(act, "hi", HI["att_" + name] + j // 2 - 1)
                    at = 0
                    for m, parts in J["flips"](j // 2, j % 2, flip_tile(name, j), Sj[0]):
                        ready(act, "lo", m)
                        r, w_ = parts[0][0], len(parts) * P
                        K(copy(Pt[0:r, at:at + w_], tile("lo", m)[0:r, 0:w_]))
                        act.sem_inc(free("lo", m), 1)
                        at += w_
                    act.sem_inc(ev("flipped"), 1)

                def out(j):
                    if j % 2:
                        h, m = j // 2, HI["att_" + name] + j // 2
                        ready(act, "hi", m)
                        copy(hf[:, J["head0"] + h, :], tile("hi", m)[:, 0:S]).then_inc(free("hi", m), 1)

                exps(0)
                for j in range(n):
                    if j + 1 < n:
                        exps(j + 1)
                    flips(j)
                    if j:
                        out(j - 1)
                out(n - 1)
                if name != "dilA":
                    K(copy(MxDn[:, 31:32], col("c")))
                    act.sem_inc(src_ready, 4)
                    split({"dilB": "dilo", "nsa": "nsao", "sb": "sbo", "moba": "mobao"}[name], hf)

            def post(name):
                for i, (ch, gain) in enumerate(PAIRS[name]):
                    k, m = POST0[name] + i, LO[name] + 2 * i
                    fn(Tb[:, 0:512], QK[:, ch:ch + 2, :].rearrange("p c s -> p (c s)"), ACT.Square).then_inc(ev("qk_sq"), 1)
                    if k:
                        act.wait_ge(ev("qk_norm"), k)
                    ready(act, "lo", m)
                    K(fn(Pt[:, 0:512], tile("lo", m), ACT.Ln, scale=1.0 / DH, bias=EPS))
                    act.sem_inc(free("lo", m), 1)
                    fn(Pt[:, 0:512], Pt[:, 0:512], ACT.Exp, scale=-0.5).then_inc(ev("qk_rs"), 1)

            def nsapost():
                act.dma_start(WC, d["wcmp"].rearrange("p (j l e) -> p j l e", j=2, l=32)).then_inc(cmp_side, 16)
                m = LO["nsagate"]
                ready(act, "lo", m)
                K(fn(GATES, tile("lo", m)[:, 0:48].rearrange("p (t n) -> p t n", t=2), ACT.Exp, scale=-1.0))
                act.sem_inc(free("lo", m), 1)
                act.sem_inc(ev("gate_exp"), 1)
                post("nsapost")
                m = HI["nsacmp"]
                ready(act, "hi", m)
                K(copy(VCMP[0:N_CMP, :], tile("hi", m)[0:N_CMP, 0:S]))
                act.sem_inc(free("hi", m), 1)
                act.sem_inc(ev("vcmp"), 1)

            def conv():
                for j in range(4):
                    q, m = Q0["conv"] + 2 * j, LO["conv"] + 2 * j
                    if j:
                        act.wait_ge(ev("conv_u"), j)
                    ready(act, "lo", m)
                    K(fn(CE[:, 0:512], tile("lo", m), ACT.Exp, scale=-1.0))
                    act.sem_inc(free("lo", m), 1)
                    act.sem_inc(ev("conv_exp"), 1)
                    prep(q + PREP)
                    prep(q + 1 + PREP)

            def conv_norm():
                act.wait_ge(ev("conv_d"), 1)
                fn(SQ, CA, ACT.Square).then_inc(ev("conv_sq"), 1)
                m = LO["convn"] + 1
                ready(act, "lo", m)
                K(fn(STD, tile("lo", m)[:, 0:S], ACT.Ln, scale=1.0 / D, bias=EPS))
                act.sem_inc(free("lo", m), 1)
                fn(RST, STD, ACT.Exp, scale=-0.5).then_inc(ev("conv_rs"), 1)
                for i in range(4):
                    act.wait_ge(ev("conv_n"), i + 1)
                    fn(CT[:, 2 * i:2 * i + 2, :], CA[:, 2 * i:2 * i + 2, :], ACT.Exp, scale=-1.0).then_inc(ev("conv_e"), 1)
                split("convo", hf)

            MASK0 = {"dilA": 0, "dilB": 8, "nsa": 16, "moba": 32}
            HALF0 = {"dilA": 0, "dilB": 4, "nsa": 8, "sb": 16, "moba": 24}

            act.dma_start(cols[:, :], d["cols"]).then_inc(cs, 16)
            act.dma_start(x[:, :, :], d["xT"].rearrange("p (c s) -> p c s", c=C)).then_inc(cs, 16)
            act.dma_start(mats[:, :], d["mats"]).then_inc(cs, 16)
            act.dma_start(rows[:, :], d["rows"]).then_inc(cs, 16)
            act.dma_start(lora2, d["lora2"]).then_inc(rw_side, 16)
            act.dma_start(rwm, d["rwm"]).then_inc(rw_side, 16)
            nc.scalar.preload_act_table_set("natural_log_exp_and_others")
            act.wait_ge(cs, CS_N)
            act.wait_ge(ev("start"), 1)
            fn(silc, col("c", 0, C), ACT.Exp, scale=-1.0).then_inc(ev("c_exp"), 1)
            steps = {"ada": lambda: (prep(0), prep(1)), "mix": mix, "rwkv": rwkv, "nsapost": nsapost, "mobapost": lambda: post("mobapost"),
                     "conv": conv, "convn": conv_norm}
            for i in range(2):
                steps[f"moe{i}"] = lambda i=i: (norm(f"cm{i}"), split(f"moe{i}", hf), route(i), accumulate(f"moe{i}"))
            for i in range(4):
                steps[f"mlp{i}"] = lambda i=i: (norm(f"ml{i}"), split(f"mlp{i}", hf), accumulate(f"mlp{i}"))
            for name in order:
                if name in steps:
                    steps[name]()
                elif name.startswith("norm_"):
                    norm(name[5:])
                    nxt = {"tm1": "dil", "at0": "nsa", "at1": "sb", "at2": "conv", "at3": "moba"}.get(name[5:])
                    if nxt:
                        split(nxt, hf)
                elif name.startswith("att_"):
                    attention(name[4:])
                elif name in ("dilA", "dilB", "nsa", "sb", "moba"):
                    if name == "dilA":
                        act.wait_ge(at_side, 16)
                    linears(name)
                else:
                    only_prep(name)

        @block.vector
        def _(dve):
            chain, own = sem("dve_chain"), [0]
            v = nc.vector
            MUL, ADD, SUB = ALU.mult, ALU.add, ALU.subtract

            def K(ins, it=None, per=0):
                own[0] += 1
                ins.then_inc(chain, 1)
                dve.wait_ge(chain, own[0] if it is None else it * per + own[0])

            def tt(out, a, b, op):
                return v.tensor_tensor(out, a, b, op)

            def ts(out, a, s1, s2, o1, o2=ALU.bypass):
                return v.tensor_scalar(out, a, s1, s2, o1, o2)

            def stt(out, a, s, b, o1, o2):
                return v.scalar_tensor_tensor(out, a, s, b, o1, o2)

            def prep(q, it=None, loop=None):
                if q >= NS:
                    return
                s = (ADA + q) % RING
                dve.wait_ge(wh_ready, q + 1 if it is None else it * loop["q"] + q + 1)
                tt(wl[:, q % PREP, :], ring[:, s, :], wh[:, q % PREP, :].bitcast(F32), SUB).then_inc(w_ready, 1)

            def split(name, src):
                k = VER[name]
                for i in range(4):
                    dve.wait_ge(hh_ready, 4 * k + i + 1)
                    tt(hl[:, 2 * i:2 * i + 2, :], src[:, 2 * i:2 * i + 2, :], hh[:, 2 * i:2 * i + 2, :].bitcast(F32), SUB)\
                        .then_inc(h_ready, 1)

            def norm(name):
                k = NORMS.index(name)
                dve.wait_ge(ev("rstd"), k + 1)
                for i in range(4):
                    for c in (2 * i, 2 * i + 1):
                        if name == "final":
                            last = stt(x[:, c, :], x[:, c, :], col("final", c), RST, MUL, MUL)
                        else:
                            g = gm[:, k, c:c + 1] if k < 4 else col(GAIN[name], c)
                            last = stt(hf[:, c, :], x[:, c, :], g, RST, MUL, MUL)
                    if k < 4:
                        K(last)
                        sh = (k % 2) * 24
                        for c in (2 * i, 2 * i + 1):
                            last = ts(hf[:, c, :], hf[:, c, :], mod[:, k // 2, sh + c:sh + c + 1], None, ADD)
                    if name == "final":
                        if i == 3:
                            last.then_inc(ev("x_ready"), 1)
                    elif name == "tm0":
                        K(last)
                    else:
                        last.then_inc(src_ready, 1)

            def residual(name, gate=None):
                q0, m0 = Q0[name], LO[name]
                for j in range(4):
                    ready(dve, "lo", m0 + j)
                    t = tile("lo", m0 + j)
                    last = add_tile(t, 2 * j, gate)
                    if j == 3:
                        K(last)
                        dve.sem_inc(free("lo", m0 + j), 1)
                        dve.sem_inc(ev("x_ready"), 1)
                    else:
                        last.then_inc(free("lo", m0 + j), 1)
                    prep(q0 + j + PREP)

            def add_tile(t, c, gate):
                if gate is None:
                    xs = x[:, c:c + 2, :].rearrange("p c s -> p (c s)")
                    return tt(xs, t, xs, ADD)
                for i in range(2):
                    g = mod[:, gate[0], gate[1] + c + i:gate[1] + c + i + 1]
                    last = stt(x[:, c + i, :], t[:, i * S:(i + 1) * S], g, x[:, c + i, :], MUL, ADD)
                return last

            def ada():
                m = LO["ada"]
                ready(dve, "lo", m)
                for i in range(2):
                    K(tt(mod[:, i, :], tile("lo", m)[:, 48 * i:48 * i + 48], col(f"ada_b{i}", 0, 48), ADD))
                dve.sem_inc(free("lo", m), 1)
                for k in range(4):
                    sc = (k % 2) * 24 + 8
                    g = col(f"norm_{('tm', 'cm')[k % 2]}{k // 2}", 0, C)
                    K(stt(gm[:, k, :], mod[:, k // 2, sc:sc + 8], 1.0, g, ADD, MUL))
                prep(0)
                prep(1)

            def mix():
                K(tt(xx, HF[:, :, 0:S], HF[:, :, 2:S + 2], ADD))
                K(stt(xx, xx, 0.5, hf, MUL, SUB))

                def mixed(j):
                    for i in range(4):
                        for c in (2 * i, 2 * i + 1):
                            last = stt(mixb[:, c, :], xx[:, c, :], col("mu", 8 * j + c), hf[:, c, :], MUL, ADD)
                        last.then_inc(src_ready, 1)
                    split(f"mix{j}", mixb)

                for j in range(3):
                    mixed(j)
                    for i in range(4):
                        prep(Q0["rkv"] + 4 * j + i + PREP)
                mixed(3)
                dve.wait_ge(ev("lora_exp"), 1)
                K(ts(lex[:, 0:S], lex[:, 0:S], 1.0, None, ADD))
                K(v.reciprocal(lex[:, 0:S], lex[:, 0:S]))
                K(ts(th[:, 0, :], lex[:, 0:S], -2.0, 1.0, MUL, ADD))
                dve.sem_inc(ev("lora_w"), 1)
                dve.sem_inc(ev("lora_ready"), 1)
                mixed(4)
                prep(Q0["lora"] + PREP)
                mixed(5)
                dve.wait_ge(ev("lora_exp"), 2)
                K(ts(lex, lex, 1.0, None, ADD))
                tg = th[:, 2:4, :].rearrange("p j s -> p (j s)")
                v.reciprocal(tg, lex).then_inc(ev("lora_ready"), 1)
                prep(Q0["lora"] + 1 + PREP)

            def rwkv():
                dve.wait_ge(rw_side, 32)
                for z in (0, 1):
                    K(v.memset(RW[z]["S0"], 0.0))
                for c in range(C):
                    T, n = rw_tiles(c), 2 * c

                    def got(*key):
                        ready(dve, "lo", T[key])
                        return tile("lo", T[key])

                    def let(ins, *key):
                        ins.then_inc(free("lo", T[key]), 1)

                    K(ts(kkc, kT[:, c, :], col("kk", c), None, MUL))
                    dve.sem_inc(ev("rw_kkc"), 1)
                    K(ts(rkr, rT[:, c, :], col("rk", c), None, MUL))
                    K(ts(kkn, got("kk")[:, 0:S], 1e-24, float(2 ** 40), ALU.max, MUL))
                    dve.sem_inc(free("lo", T[("kk",)]), 1)
                    dve.sem_inc(ev("rw_kkm"), 1)
                    for z in (0, 1):
                        b = RW[z]
                        dve.wait_ge(ev("rw_ea"), n + z + 1)
                        K(ts(b["ea"], b["ea"], 1.0, None, ADD))
                        K(v.reciprocal(b["ea"], b["ea"]))
                        K(ts(b["cx"], b["ea"][:, 0:S], -HALF_LOG, None, MUL))
                        for j in range(2):
                            a = slice(j * P, (j + 1) * P)
                            o, i_ = b["cum"][:, a], b["cx"][:, a]
                            if z:
                                o, i_ = o[:, ::-1], i_[:, ::-1]
                            last = v.tensor_tensor_scan(o, ones, i_, 0.0, MUL, ADD)
                        K(last)
                        for j in range(2):
                            a, mid = slice(j * P, (j + 1) * P), j * P + 63
                            last = ts(b["cc"][:, a], b["cum"][:, a], b["cum"][:, mid:mid + 1], None, SUB)
                        K(last)
                        tt(b["cx"], b["cc"], b["cx"], SUB)
                        e, mo = (P - 1, P + 63) if z == 0 else (P, 63)
                        tt(b["fac"][:, 0:1], b["cc"][:, e:e + 1], b["cum"][:, mo:mo + 1], ADD).then_inc(ev("rw_cc"), 1)
                    dve.wait_ge(ev("rw_kkn"), c + 1)
                    K(stt(kkc, kkc, float(2 ** 20), kkn, MUL, MUL))
                    for z in (0, 1):
                        b = RW[z]
                        dve.wait_ge(ev("rw_E"), n + z + 1)
                        E1, E2, E3 = (b["E"][:, i * S:(i + 1) * S] for i in range(3))
                        K(ts(b["cum"], b["ea"][:, S:2 * S], col("ka", c), omka[:, c:c + 1], MUL, ADD))
                        K(tt(b["cum"], b["cum"], kT[:, c, :], MUL))
                        K(tt(b["cc"], kkc, b["ea"][:, S:2 * S], MUL))
                        tt(b["ar"][:, S:2 * S], rT[:, c, :], E2, MUL)
                        stt(b["ar"][:, 0:S], kkc, -1.0, E1, MUL, MUL)
                        tt(b["kt"], b["cum"], E3, MUL)
                        tt(b["cx"], b["cum"], rkr, MUL)
                        tt(b["bt"], b["cc"], E3, MUL).then_inc(ev("rw_feat"), 1)
                    for z in (0, 1):
                        b = RW[z]
                        low = "low" if z else "up"
                        incl, strict = rmask("li" if z else "ui"), rmask("ls" if z else "us")

                        def two(m):
                            return m[:, None, :].to_broadcast([P, 2, P])

                        def part(name, h):
                            return b[name][:, h * S:(h + 1) * S].rearrange("p (j t) -> p j t", j=2)

                        for h in (0, 1):
                            t = got(f"B{h}", z).rearrange("p (j i t) -> p j i t", j=2, i=2)
                            tt(part("X", h), t[:, :, 0, :], two(rmask(low + "0")), MUL)
                            tt(part("N6", h), t[:, :, 0, :], two(rmask(low + "6")), MUL)
                            let(tt(part("Arb", h), t[:, :, 1, :], two(incl), MUL), f"B{h}", z)
                        for h in (0, 1):
                            t = got(f"K{h}", z).rearrange("p (j i t) -> p j i t", j=2, i=2)
                            tt(part("Aak", h), t[:, :, 0, :], two(strict), MUL)
                            let(tt(part("Ark", h), t[:, :, 1, :], two(incl), MUL), f"K{h}", z)
                        X4 = b["X"].rearrange("p (q t) -> p q t", q=4)
                        dve.wait_ge(free("lo", T[("K1", z)]), T[("K1", z)] // 4 + 1)
                        tt(X4, X4, ident[:, None, :].to_broadcast([P, 4, P]), ADD).then_inc(ev("rw_x"), 1)
                    for lev in range(1, RW_LEVELS + 1):
                        for z in (0, 1):
                            b = RW[z]
                            if lev == 1:
                                dve.wait_ge(ev("rw_al"), 12 * c + 2 * z + 1)
                                dve.wait_ge(ev("rw_x"), n + z + 1)
                            t = got("X", lev, z)
                            K(tt(b["X"], t, b["X"], ADD))
                            dve.sem_inc(free("lo", T[("X", lev, z)]), 1)
                            if lev < RW_LEVELS:
                                t = got("Y", lev, z)
                                K(tt(b["Y"], t, b["Y"], ADD))
                                dve.sem_inc(free("lo", T[("Y", lev, z)]), 1)
                            dve.sem_inc(ev("rw_xy"), 1)
                    for ji in (0, 1):
                        for z in (0, 1):
                            b = RW[z]
                            dve.wait_ge(ev("rw_z"), (c * 2 + ji) * 2 + z + 1)
                            K(tt(b["R"], got("R", ji, z)[:, 0:P], b["Z"], ADD))
                            dve.sem_inc(free("lo", T[("R", ji, z)]), 1)
                            dve.sem_inc(ev("rw_r"), 1)
                        if ji == 0:
                            for z in (0, 1):
                                b = RW[z]
                                t = got("S", z)
                                for h in (0, 1):
                                    r = slice(64 * h, 64 * h + 64)
                                    last = ts(b["S0"][r, r], t[r, 0:64], b["fac"][r, 1:2], None, MUL)
                                K(last)
                                dve.sem_inc(free("lo", T[("S", z)]), 1)
                                dve.sem_inc(ev("rw_s"), 1)
                    for z in (0, 1):
                        b = RW[z]
                        dve.wait_ge(ev("rw_ys"), n + z + 1)
                        K(stt(b["cc"], got("mean", z)[:, 0:S], -1.0 / 64, b["cum"], MUL, ADD))
                        dve.sem_inc(free("lo", T[("mean", z)]), 1)
                        dve.sem_inc(ev("rw_d"), 1)
                    for z in (0, 1):
                        b = RW[z]
                        dve.wait_ge(ev("rw_rs"), n + z + 1)
                        K(tt(b["cum"], b["cc"], b["E"][:, S:2 * S], MUL))
                        K(ts(b["cum"], b["cum"], col("lnw", c), col("lnb", c), MUL, ADD))
                        m = HI["rwkv"] + 4 * c + z
                        ready(dve, "hi", m)
                        E3 = b["E"][:, 2 * S:3 * S]
                        K(tt(E3, tile("hi", m)[:, 0:S], vT[:, c, :], MUL))
                        dve.sem_inc(free("hi", m), 1)
                        K(tt(b["cum"], b["cum"], E3, ADD))
                        t = got("g", z)[:, 0:S]
                        if z == 0:
                            K(tt(rT[:, c, :], b["cum"], t, MUL))
                        else:
                            K(tt(b["cum"], b["cum"], t, MUL))
                        dve.sem_inc(free("lo", T[("g", z)]), 1)
                        if z:
                            K(tt(rT[:, c, :], rT[:, c, :], b["cum"], ADD))
                dve.sem_inc(src_ready, 4)
                dve.sem_inc(ev("rwkv_done"), 1)
                split("rwo", rT)

            def route(i):
                m = LO[f"route{i}"]
                ready(dve, "lo", m)
                K(v.tensor_copy(Lr, tile("lo", m)[:, 0:72].rearrange("p (t n) -> p t n", t=2)))
                dve.sem_inc(free("lo", m), 1)
                at = [16]

                def tmp(*shape):
                    n = int(np.prod(shape))
                    a = MO[:, at[0]:at[0] + n]
                    at[0] += n
                    if len(shape) == 2:
                        a = a.rearrange("p (a b) -> p a b", a=shape[0])
                    return a

                def wide(a, n):
                    return a[:, :, None].to_broadcast([P, 2, n]) if len(a.shape) == 2 else a.to_broadcast([P, 2, n])

                def first_of(src, best, n):
                    eq, cum, one = tmp(2, n), tmp(2, n), tmp(2, n)
                    K(tt(eq, src, wide(best, n), ALU.is_equal))
                    for t in range(2):
                        last = v.tensor_tensor_scan(cum[:, t, :], ones[:, 0:n], eq[:, t, :], 0.0, MUL, ADD)
                    K(last)
                    K(stt(one, cum, 1.0, eq, ALU.is_equal, MUL))
                    return one

                gl = Lr[:, :, 0:4]
                mg, sg = tmp(2), tmp(2)
                K(v.reduce_max(mg, gl, AX_X))
                e4 = MO[:, 0:8].rearrange("p (t n) -> p t n", t=2)
                tt(e4, gl, wide(mg, 4), SUB).then_inc(ev("group_arg"), 1)
                og = first_of(gl, mg, 4)
                dve.wait_ge(ev("group_exp"), i + 1)
                K(v.tensor_reduce(sg, e4, AX_X, ADD))
                K(v.reciprocal(sg, sg))
                es, t8 = tmp(2, 8), tmp(2, 8)
                for g in range(4):
                    K(tt(t8 if g else es, Lr[:, :, 4 + 8 * g:12 + 8 * g], og[:, :, g:g + 1].to_broadcast([P, 2, 8]), MUL))
                    if g:
                        K(tt(es, es, t8, ADD))
                m1, m2 = tmp(2), tmp(2)
                K(v.reduce_max(m1, es, AX_X))
                o1 = first_of(es, m1, 8)
                e2 = tmp(2, 8)
                K(stt(e2, o1, NEG, es, MUL, ADD))
                K(v.reduce_max(m2, e2, AX_X))
                tt(MO[:, 8:10], m2, m1, SUB).then_inc(ev("pair_arg"), 1)
                o2 = first_of(e2, m2, 8)
                dve.wait_ge(ev("pair_exp"), i + 1)
                w1, w2 = tmp(2), tmp(2)
                K(ts(w1, MO[:, 8:10], 1.0, None, ADD))
                K(v.reciprocal(w1, w1))
                K(tt(w1, w1, sg, MUL))
                K(tt(w2, w1, MO[:, 8:10], MUL))
                inner = tmp(2, 8)
                K(tt(inner, o1, wide(w1, 8), MUL))
                K(tt(t8, o2, wide(w2, 8), MUL))
                K(tt(inner, inner, t8, ADD))
                for g in range(4):
                    last = tt(Gt[:, :, 8 * g:8 * g + 8], inner, og[:, :, g:g + 1].to_broadcast([P, 2, 8]), MUL)
                last.then_inc(ev("gates"), 1)
                dve.wait_ge(ev("gates_wide"), i + 1)

            def accumulate(name):
                moe = name[:3] == "moe"
                ups, n, per = (2, EXPERTS, 8) if moe else (1, UNITS, 4)
                q0, m0, d0 = Q0[name], LO[name], DOWN0[name]
                loop = {"lo": per, "down": 4, "q": 4 * (ups + 1)}
                kper = 4 * (5 if moe else 1)

                def w(sem_, val, it, per_):
                    dve.wait_ge(sem_, val if it is None else it * per_ + val)

                def hidden(e, m, it):
                    u = e % 2
                    hid = HID0[name] + e
                    if moe:
                        i = hid if name == "moe0" else hid
                        w(ev("hid_exp"), hid + 1, it, 4)
                        T = T0[:, u, :]
                        K(ts(T, T, 1.0, None, ADD), it, kper)
                        K(v.reciprocal(T, T), it, kper)
                        K(tt(T, T, tile("lo", m), MUL), it, kper)
                        dve.sem_inc(free("lo", m), 1)
                        w(tile_ready["lo"], m + 2, it, per)
                        K(tt(T, T, tile("lo", m + 1), MUL), it, kper)
                        dve.sem_inc(free("lo", m + 1), 1)
                        g = GB[:, e, :] if it is None else GB[:, bass.ds(it * 4 + e, 1), :].rearrange("p e s -> p (e s)")
                        K(tt(T1.rearrange("p (f s) -> p f s", f=2), T.rearrange("p (f s) -> p f s", f=2),
                             g[:, None, :].to_broadcast([P, 2, S]), MUL), it, kper)
                        dve.sem_inc(ev("hid_wide"), 1)
                    w(ev("hidh_ready"), hid + 1, it, 4)
                    tt(hidl[:, u, :], T1 if moe else T0[:, u, :], hidh[:, u, :].bitcast(F32), SUB).then_inc(ev("hidden"), 1)

                def step(e, it=None):
                    b = q0 + ups + e * (ups + 1)
                    if e + 1 < n:
                        for u in range(ups):
                            prep(b + u + PREP, it, loop)
                        hidden(e + 1, m0 + ups * (e + 1), it)
                        prep(b + ups + PREP, it, loop)
                    else:
                        prep(b + PREP, it, loop)

                for u in range(ups):
                    prep(q0 + u + PREP)
                hidden(0, m0, None)
                first = own[0]
                with dve.Fori(0, n // 4 - 1) as it:
                    for e in range(4):
                        step(e, it)
                kk_ = own[0] - first
                assert kk_ == (kper if moe else 0), kk_
                own[0] = first + kk_ * (n // 4 - 1)
                for e in range(n - 4, n):
                    step(e)
                for i in range(4):
                    m = HI[name] + i
                    ready(dve, "hi", m)
                    last = add_tile(tile("hi", m), 2 * i, (int(name[3]), 40) if moe else None)
                    if i < 3:
                        last.then_inc(free("hi", m), 1)
                    else:
                        K(last)
                        dve.sem_inc(free("hi", m), 1)
                        dve.sem_inc(ev("x_ready" if name != "mlp3" else "result_ready"), 1)

            def only_prep(name):
                for j in range(dict(ORDER)[name]):
                    prep(Q0[name] + j + PREP)

            def attention(name):
                J = ATT[name]
                b0, n = J["first"], J["jobs"]

                def m_(j):
                    return score_tile(name, j)

                def masked(j):
                    h, qt = j // 2, j % 2
                    s = Sj[(b0 + j) % 2]
                    if j >= 2:
                        ready(dve, "lo", flip_tile(name, j - 2) + J["lo"] // 2 - 1)
                    m = m_(j)
                    qs = slice(qt * S, (qt + 1) * S)
                    if name in ("dilA", "dilB"):
                        for g in range(3):
                            sl = -SLOPES[g * HEADS + J["head0"] + h]
                            last = stt(Tb[:, g * S:(g + 1) * S], amask("dist")[:, qs], sl, amask(f"dil{g}")[:, qs], MUL, ADD)
                        K(last)
                        ready(dve, "lo", m)
                        stt(s[:, 0:512], tile("lo", m), SCALE, Tb[:, 0:512], MUL, ADD).then_inc(free("lo", m), 1)
                        ready(dve, "lo", m + 1)
                        K(stt(s[:, 512:768], tile("lo", m + 1)[:, 0:S], SCALE, Tb[:, 512:768], MUL, ADD))
                        dve.sem_inc(free("lo", m + 1), 1)
                    elif name == "nsa":
                        ready(dve, "lo", m)
                        cm = amask("causal")[:, qs][:, None, :].to_broadcast([P, 2, S])
                        stt(s[:, 0:512].rearrange("p (a b) -> p a b", a=2), tile("lo", m).rearrange("p (a b) -> p a b", a=2),
                            SCALE, cm, MUL, ADD).then_inc(free("lo", m), 1)
                        ready(dve, "lo", m + 1)
                        K(stt(s[:, 512:512 + N_CMP], tile("lo", m + 1)[:, 0:N_CMP], SCALE,
                              amask("cmpadd")[:, 16 * qt:16 * qt + N_CMP], MUL, ADD))
                        dve.sem_inc(free("lo", m + 1), 1)
                    else:
                        ready(dve, "lo", m)
                        K(stt(s[:, 0:S], tile("lo", m)[:, 0:S], SCALE, amask("causal")[:, qs], MUL, ADD))
                        dve.sem_inc(free("lo", m), 1)
                    o = 16 * ((b0 + j) % 2)
                    for i, (a, b) in enumerate(J["soft"]):
                        last = v.reduce_max(MxDn[:, o + i:o + i + 1], s[:, a:b], AX_X, negate=True)
                    last.then_inc(ev("masked"), 1)

                def scaled(j):
                    h, qt = j // 2, j % 2
                    s = Sj[(b0 + j) % 2]
                    dve.wait_ge(ev("exped"), MASK0[name] + j + 1)
                    o, ng = 16 * ((b0 + j) % 2), len(J["soft"])
                    K(v.reciprocal(MxDn[:, o + 8:o + 8 + ng], MxDn[:, o + 4:o + 4 + ng]))
                    if name == "nsa":
                        gs = GATES[:, qt, :].rearrange("p (b h) -> p b h", b=3)
                        for i, br in enumerate((1, 2, 0)):
                            last = tt(MxDn[:, o + 8 + i:o + 9 + i], MxDn[:, o + 8 + i:o + 9 + i], gs[:, br, h:h + 1], MUL)
                        K(last)
                        K(tt(s[:, 512:512 + N_CMP], s[:, 512:512 + N_CMP], amask("cmpmul")[:, 16 * qt:16 * qt + N_CMP], MUL))
                    for i, (a, b) in enumerate(J["soft"]):
                        last = ts(s[:, a:b], s[:, a:b], MxDn[:, o + 8 + i:o + 9 + i], None, MUL)
                    last.then_inc(ev("probs"), 1)

                if name == "sb":
                    for j in range(n):
                        qt, s, m = j % 2, Sj[(b0 + j) % 2], m_(j)
                        qs = slice(qt * S, (qt + 1) * S)
                        if j >= 2:
                            ready(dve, "lo", flip_tile(name, j - 2) + J["lo"] // 2 - 1)
                        z = tile("lo", m)[:, 0:S]
                        dve.wait_ge(ev("sb_log"), j + 1)
                        K(ts(s[:, 0:S], z, SCALE, 0.0, MUL, ALU.max))
                        K(tt(s[:, 0:S], s[:, 0:S], Ub[:, 0:S], ADD))
                        K(stt(s[:, 0:S], s[:, 0:S], -1.0, amask("strict")[:, qs], MUL, MUL))
                        K(v.tensor_tensor_scan(Ab_[:, ::-1], ones[:, 0:1].to_broadcast([P, S]), s[:, 0:S][:, ::-1], 0.0, MUL, ADD))
                        K(stt(s[:, 0:S], z, SCALE, Ab_, MUL, ADD))
                        dve.sem_inc(free("lo", m), 1)
                        tt(s[:, 0:S], s[:, 0:S], amask("strictadd")[:, qs], ADD).then_inc(ev("sb_arg"), 1)
                    return
                masked(0)
                for j in range(n):
                    if j + 1 < n:
                        masked(j + 1)
                    scaled(j)

            def post(name):
                pairs = PAIRS[name]
                for i, (ch, gain) in enumerate(pairs):
                    k, m = POST0[name] + i, LO[name] + 2 * i + 1
                    qk = QK[:, ch:ch + 2, :]
                    flat = qk.rearrange("p c s -> p (c s)")
                    dve.wait_ge(ev("qk_rs"), k + 1)
                    K(stt(Ub[:, 0:512], flat, col(*gain), Pt[:, 0:512], MUL, MUL))
                    dve.sem_inc(ev("qk_norm"), 1)
                    cos, sin = (amask(a)[:, None, :].to_broadcast([P, 2, S]) for a in ("cos", "sin"))
                    tt(qk, Ub[:, 0:512].rearrange("p (c s) -> p c s", c=2), cos, MUL)
                    ready(dve, "lo", m)
                    t2 = Rb[:, 0:512]
                    K(tt(t2.rearrange("p (c s) -> p c s", c=2), tile("lo", m).rearrange("p (c s) -> p c s", c=2), sin, MUL))
                    dve.sem_inc(free("lo", m), 1)
                    K(tt(flat, flat, t2, ADD))

            def nsapost():
                dve.wait_ge(ev("gate_exp"), 1)
                K(ts(GATES, GATES, 1.0, None, ADD))
                K(v.reciprocal(GATES, GATES))
                post("nsapost")
                pos = [col("cmp_pos", 32 * j, 32) for j in range(2)]
                for j, ch in ((0, 8), (1, 10)):
                    for g in range(2):
                        base = QK[:, ch + g, :]
                        for hf_ in range(2):
                            src = base.rearrange("p (n l) -> p l n", l=16)[:, :, hf_:hf_ + N_CMP]
                            last = tt(KP[:, j, 16 * hf_:16 * hf_ + 16, g, :], src,
                                      pos[j][:, 16 * hf_:16 * hf_ + 16, None].to_broadcast([P, 16, N_CMP]), ADD)
                last.then_inc(ev("kp"), 1)
                m = LO["nsacmp"]
                ready(dve, "lo", m)
                K(v.tensor_copy(CMP.rearrange("p (g n) -> p g n", g=2)[:, :, 0:N_CMP],
                                tile("lo", m)[:, 0:2 * N_CMP].rearrange("p (g n) -> p g n", g=2)))
                dve.sem_inc(free("lo", m), 1)
                dve.wait_ge(ev("vcmp"), 1)
                dve.sem_inc(ev("qkv_done"), 1)

            def conv():
                K(v.memset(CU[:, :, 0:30], 0.0))
                for j in range(4):
                    q, m = Q0["conv"] + 2 * j, LO["conv"] + 2 * j
                    dve.wait_ge(ev("conv_exp"), j + 1)
                    prep(q + PREP)
                    E_ = CE[:, 0:512]
                    K(ts(E_, E_, 1.0, None, ADD))
                    K(v.reciprocal(E_, E_))
                    ready(dve, "lo", m + 1)
                    K(tt(CU[:, 2 * j:2 * j + 2, 30:286], E_.rearrange("p (c s) -> p c s", c=2),
                         tile("lo", m + 1).rearrange("p (c s) -> p c s", c=2), MUL))
                    dve.sem_inc(free("lo", m + 1), 1)
                    dve.sem_inc(ev("conv_u"), 1)
                    prep(q + 1 + PREP)
                for c in range(C):
                    last = ts(CA[:, c, :], CU[:, c, 0:S], col("dw_w", c), col("dw_b", c), MUL, ADD)
                K(last)
                for w in range(1, CONV_W):
                    for c in range(C):
                        last = stt(CA[:, c, :], CU[:, c, w:w + S], col("dw_w", C * w + c), CA[:, c, :], MUL, ADD)
                    K(last)
                dve.sem_inc(ev("conv_out"), 1)

            def conv_norm():
                m = LO["convn"]
                ready(dve, "lo", m)
                mb = tile("lo", m)[:, 0:S][:, None, :].to_broadcast([P, C, S])
                K(stt(CA, mb, -1.0 / D, CA, MUL, ADD))
                dve.sem_inc(free("lo", m), 1)
                dve.sem_inc(ev("conv_d"), 1)
                dve.wait_ge(ev("conv_rs"), 1)
                for i in range(4):
                    for c in (2 * i, 2 * i + 1):
                        last = stt(CA[:, c, :], CA[:, c, :], col("cln_g", c), RST, MUL, MUL)
                    K(last)
                    for c in (2 * i, 2 * i + 1):
                        last = ts(CA[:, c, :], CA[:, c, :], col("cln_b", c), None, ADD)
                    K(last)
                    dve.sem_inc(ev("conv_n"), 1)
                for i in range(4):
                    dve.wait_ge(ev("conv_e"), i + 1)
                    a = slice(2 * i, 2 * i + 2)
                    K(ts(CT[:, a, :], CT[:, a, :], 1.0, None, ADD))
                    K(v.reciprocal(CT[:, a, :], CT[:, a, :]))
                    tt(hf[:, a, :], CA[:, a, :], CT[:, a, :], MUL).then_inc(src_ready, 1)
                split("convo", hf)

            MASK0 = {"dilA": 0, "dilB": 8, "nsa": 16, "moba": 32}

            v.memset(zero[:, :], 0.0)
            v.memset(HF[:, :, 0:1], 0.0)
            K(v.memset(HF[:, :, 257:258], 0.0))
            dve.wait_ge(cs, CS_N)
            ts(neg0[:, 0:16], col("w0", 0, 16), -1.0, None, MUL)
            ts(neg0[:, 16:32], col("a0", 0, 16), -1.0, None, MUL)
            K(ts(omka, col("ka", 0, C), -1.0, 1.0, MUL, ADD))
            dve.sem_inc(ev("start"), 1)
            dve.wait_ge(ev("c_exp"), 1)
            K(ts(silc, silc, 1.0, None, ADD))
            K(v.reciprocal(silc, silc))
            tt(silc, silc, col("c", 0, C), MUL).then_inc(ev("silu_c"), 1)
            gates = {"rwo": (0, 16), "dilo": (1, 16)}
            steps = {"ada": ada, "mix": mix, "rwkv": rwkv, "nsapost": nsapost,
                     "mobapost": lambda: (post("mobapost"), dve.sem_inc(ev("qkv_done"), 1)), "conv": conv, "convn": conv_norm}
            for i in range(2):
                steps[f"moe{i}"] = lambda i=i: (norm(f"cm{i}"), split(f"moe{i}", hf), route(i), accumulate(f"moe{i}"))
            for i in range(4):
                steps[f"mlp{i}"] = lambda i=i: (norm(f"ml{i}"), split(f"mlp{i}", hf), accumulate(f"mlp{i}"))
            for name in order:
                if name in steps:
                    steps[name]()
                elif name.startswith("norm_"):
                    norm(name[5:])
                    nxt = {"tm1": "dil", "at0": "nsa", "at1": "sb", "at2": "conv", "at3": "moba"}.get(name[5:])
                    if nxt:
                        split(nxt, hf)
                elif name.startswith("att_"):
                    attention(name[4:])
                    nxt = {"dilB": "dilo", "nsa": "nsao", "sb": "sbo", "moba": "mobao"}.get(name[4:])
                    if nxt:
                        split(nxt, hf)
                elif name in ("dilA", "dilB", "nsa", "sb", "moba"):
                    if name == "dilA":
                        dve.wait_ge(at_side, 16)
                    only_prep(name)
                else:
                    residual(name, gates.get(name))
            if stop:
                K(v.memset(small[:, 0:1], 0.0))
                dve.sem_inc(ev("result_ready"), 1)

        @block.gpsimd
        def _(pool):
            chain, own = sem("pool_chain"), [0]

            def K(ins):
                own[0] += 1
                ins.then_inc(chain, 1)
                pool.wait_ge(chain, own[0])

            def masked(b, name, z, lev):
                low = "up" if z else "low"
                m = rmask(f"{low}{lev}")[:, None, :].to_broadcast([P, 4, P])
                return nc.gpsimd.tensor_tensor(b[name].rearrange("p (q t) -> p q t", q=4), b["A"].rearrange("p (q t) -> p q t", q=4),
                                               m, ALU.mult)

            if "rwkv" in order:
                pool.wait_ge(cs, CS_N)
                pool.wait_ge(rw_side, 32)
                for c in range(C):
                    T = rw_tiles(c)
                    for z in (0, 1):
                        b = RW[z]
                        pool.wait_ge(ev("rw_A"), 2 * c + z + 1)
                        K(masked(b, "Y", z, 0))
                        Y4 = b["Y"].rearrange("p (q t) -> p q t", q=4)
                        nc.gpsimd.tensor_tensor(Y4, Y4, ident[:, None, :].to_broadcast([P, 4, P]), ALU.add).then_inc(ev("rw_al"), 1)
                        masked(b, "Al", z, 1).then_inc(ev("rw_al"), 1)
                    for lev in range(2, RW_LEVELS + 1):
                        for z in (0, 1):
                            ready(pool, "lo", T[("W", lev - 1, z)])
                            masked(RW[z], "Al", z, lev).then_inc(ev("rw_al"), 1)


def kernel(**inputs):
    from concourse import bacc
    from concourse.bass_utils import run_bass_kernel_spmd

    arrays = arrange(inputs)
    arrays.update(mats=MATS_A, rwm=RWM_A, atm=ATM_A)
    nc = bacc.Bacc("TRN2", target_bir_lowering=False, num_devices=1)
    d = {n: nc.dram_tensor("in_" + n, a.shape, F32, kind="ExternalInput").ap() for n, a in arrays.items()}
    out = nc.dram_tensor("out", (P, C, S), F32, kind="ExternalOutput").ap()
    build(nc, d, out, *STOP)
    r = run_bass_kernel_spmd(nc, [{"in_" + n: a for n, a in arrays.items()}], core_ids=[0])
    o = np.asarray(r.results[0]["out"]).reshape(P, C, S)
    return np.ascontiguousarray(o.transpose(2, 1, 0).reshape(1, S, D))


STOP = ()
```
